# Optimizing a Trainium2 kernel written in Bass

```python
import math
import jax, jax.numpy as jnp
from jax import lax
import numpy as np

D_MODEL = 1024
BATCH = 1
SEQ = 512
DEPTH = 1

HEAD_DIM = 64
RMS_EPS = 1e-6
DSWA_PATTERNS = ((128, 1), (512, 4), (2048, 16))
DSWA_HEADS_PER_GROUP = 4
DSWA_HEADS = len(DSWA_PATTERNS) * DSWA_HEADS_PER_GROUP
DSWA_BLOCK = 128
A_WIDTH = DSWA_HEADS * HEAD_DIM
GLA_HEADS = 4
GLA_DK = D_MODEL // 2 // GLA_HEADS
GLA_DV = D_MODEL // GLA_HEADS
GLA_GATE_RANK = 16
GLA_TAU = 16.0
GLA_CHUNK = 64
DSA_HEADS = 12
IDX_HEADS = 8
IDX_DIM = 64
IDX_TOPK = 256
DSA_QBLOCK = 128
REL_BUCKETS = 32
REL_MAX_DIST = 2048
N_BIAS_HEADS = DSWA_HEADS + DSA_HEADS
D_FF = -(-8 * D_MODEL // (3 * 256)) * 256
PLE_DIM = 256
_IN_WIDTHS = (
    A_WIDTH, A_WIDTH, A_WIDTH,
    GLA_HEADS * GLA_DK, GLA_HEADS * GLA_DK,
    GLA_HEADS * GLA_DV, GLA_HEADS * GLA_DV, GLA_GATE_RANK,
    DSA_HEADS * HEAD_DIM, HEAD_DIM, HEAD_DIM,
    IDX_HEADS * IDX_DIM, IDX_DIM, IDX_HEADS,
)
N_IN = sum(_IN_WIDTHS)
_IN_OFFSETS = tuple(sum(_IN_WIDTHS[:i + 1]) for i in range(len(_IN_WIDTHS) - 1))

kernel_name = "hybrid_dswa_gla_dsa_gated_block"

def rms_norm(x, g):
    xf = x.astype(jnp.float32)
    y = xf * lax.rsqrt(jnp.mean(xf * xf, axis=-1, keepdims=True) + RMS_EPS)
    return (y * g.astype(jnp.float32)).astype(x.dtype)

def rel_bucket(dist):
    max_exact = REL_BUCKETS // 2
    d = jnp.maximum(dist, 0)
    df = jnp.maximum(d, 1).astype(jnp.float32)
    large = max_exact + (jnp.log(df / max_exact) / math.log(REL_MAX_DIST / max_exact)
                         * (REL_BUCKETS - max_exact)).astype(jnp.int32)
    large = jnp.minimum(large, REL_BUCKETS - 1)
    return jnp.where(d < max_exact, d, large)

def dilated_window_group(q, k, v, bias_tab, window, dilation):
    B_, S_, H, Dh = q.shape
    r = dilation
    n = window // dilation
    blk = DSWA_BLOCK
    L = S_ // r
    nblk = -(-L // blk)
    Lp = nblk * blk

    def to_res(t):
        return t.reshape(B_, L, r, H, Dh).transpose(0, 2, 1, 3, 4)

    qr = jnp.pad(to_res(q), ((0, 0), (0, 0), (0, Lp - L), (0, 0), (0, 0)))
    kv_pad = ((0, 0), (0, 0), (blk, Lp - L), (0, 0), (0, 0))
    kr = jnp.pad(to_res(k), kv_pad)
    vr = jnp.pad(to_res(v), kv_pad)
    qb = qr.reshape(B_, r, nblk, blk, H, Dh)

    def band(t):
        tb = t.reshape(B_, r, nblk + 1, blk, H, Dh)
        return jnp.concatenate([tb[:, :, :-1], tb[:, :, 1:]], axis=3)

    kb, vb = band(kr), band(vr)
    iq = jnp.arange(blk)[:, None]
    jk = jnp.arange(2 * blk)[None, :]
    delta = iq - jk + blk
    key_idx = jnp.arange(nblk)[:, None, None] * blk + jk[None] - blk
    valid = (delta >= 0) & (delta <= n) & (key_idx >= 0)
    bias = bias_tab[rel_bucket(delta * r)].transpose(2, 0, 1)
    s = jnp.einsum('brnqhd,brnkhd->brnhqk', qb, kb).astype(jnp.float32) + bias.astype(jnp.float32)
    s = jnp.where(valid[:, None], s, -jnp.inf)
    m = jnp.max(s, axis=-1)
    pexp = jnp.exp(s - m[..., None])
    l = jnp.sum(pexp, axis=-1)
    m = m.transpose(0, 1, 2, 4, 3)
    l = l.transpose(0, 1, 2, 4, 3)
    o = jnp.einsum('brnhqk,brnkhd->brnqhd', pexp, vb.astype(jnp.float32)) / l[..., None]

    def from_res(t):
        rest = t.shape[4:]
        t = t.reshape((B_, r, Lp) + rest)[:, :, :L]
        return jnp.swapaxes(t, 1, 2).reshape((B_, S_) + rest)

    return from_res(o), from_res(m), from_res(l)

def mixer_dilated(q, k, v, bias_tab):
    outs, ms, ls = [], [], []
    for g, (window, dilation) in enumerate(DSWA_PATTERNS):
        sl = slice(g * DSWA_HEADS_PER_GROUP, (g + 1) * DSWA_HEADS_PER_GROUP)
        o, m, l = dilated_window_group(q[:, :, sl], k[:, :, sl], v[:, :, sl], bias_tab[:, sl], window, dilation)
        outs.append(o)
        ms.append(m)
        ls.append(l)
    o = jnp.stack(outs)
    m = jnp.stack(ms)
    l = jnp.stack(ls)
    wts = l * jnp.exp(m - jnp.max(m, axis=0, keepdims=True))
    wts = wts / jnp.sum(wts, axis=0, keepdims=True)
    return jnp.sum(wts[..., None] * o, axis=0)

def mixer_gla(q, k, v, a_low, w_a2, b_a):
    B_, S_, H, dk = q.shape
    dv = v.shape[-1]
    C = GLA_CHUNK
    N = S_ // C
    log_a = jax.nn.log_sigmoid((a_low @ w_a2 + b_a).astype(jnp.float32)) / GLA_TAU
    bcum = jnp.cumsum(log_a.reshape(B_, N, C, H, dk), axis=2)
    qf = q.astype(jnp.float32).reshape(B_, N, C, H, dk) * dk ** -0.5
    kf = k.astype(jnp.float32).reshape(B_, N, C, H, dk)
    vf = v.astype(jnp.float32).reshape(B_, N, C, H, dv)
    b_last = bcum[:, :, -1:]
    q_in = qf * jnp.exp(bcum)
    k_in = kf * jnp.exp(-bcum)
    k_end = kf * jnp.exp(b_last - bcum)
    causal = jnp.tril(jnp.ones((C, C), dtype=bool))
    att = jnp.einsum('bnqhd,bnkhd->bnhqk', q_in, k_in)
    att = jnp.where(causal, att, 0.0)
    o_intra = jnp.einsum('bnhqk,bnkhe->bnqhe', att, vf)

    def step(state, xs):
        qc, kc, vc, dec = xs
        o = jnp.einsum('bqhd,bhde->bqhe', qc, state)
        state = state * dec[..., None] + jnp.einsum('bkhd,bkhe->bhde', kc, vc)
        return state, o

    xs = (jnp.moveaxis(q_in, 1, 0), jnp.moveaxis(k_end, 1, 0), jnp.moveaxis(vf, 1, 0),
          jnp.moveaxis(jnp.exp(b_last[:, :, 0]), 1, 0))
    state0 = jnp.zeros((B_, H, dk, dv), jnp.float32)
    _, o_inter = lax.scan(step, state0, xs)
    o = o_intra + jnp.moveaxis(o_inter, 0, 1)
    return o.reshape(B_, S_, H, dv)

def mixer_dsa(q, k, v, iq, ik, iw, bias_tab):
    B_, S_, H, Dh = q.shape
    topk = min(IDX_TOPK, S_ // 4)
    nb = S_ // DSA_QBLOCK
    pos = jnp.arange(S_)
    ikf = ik.astype(jnp.float32)
    idx_scale = (IDX_HEADS ** -0.5) * (IDX_DIM ** -0.5)

    def blocks(t):
        return jnp.swapaxes(t.reshape((B_, nb, DSA_QBLOCK) + t.shape[2:]), 0, 1)

    def one_block(args):
        qb, iqb, iwb, tq = args
        sc = jax.nn.relu(jnp.einsum('bqhd,bsd->bqhs', iqb.astype(jnp.float32), ikf))
        score = jnp.einsum('bqh,bqhs->bqs', iwb.astype(jnp.float32) * idx_scale, sc)
        visible = pos[None, :] <= tq[:, None]
        score = jnp.where(visible[None], score, -jnp.inf)
        top_s, idx = lax.top_k(score, topk)
        sel_ok = top_s > -jnp.inf
        kg = jax.vmap(lambda kk, ii: kk[ii])(k, idx)
        vg = jax.vmap(lambda vv, ii: vv[ii])(v, idx)
        logits = jnp.einsum('bqhd,bqkd->bhqk', qb, kg).astype(jnp.float32)
        bias = bias_tab[rel_bucket(tq[None, :, None] - idx)].astype(jnp.float32)
        logits = logits + bias.transpose(0, 3, 1, 2)
        logits = jnp.where(sel_ok[:, None], logits, -jnp.inf)
        prob = jax.nn.softmax(logits, axis=-1)
        return jnp.einsum('bhqk,bqkd->bqhd', prob, vg.astype(jnp.float32))

    out = lax.map(one_block, (blocks(q), blocks(iq), blocks(iw), pos.reshape(nb, DSA_QBLOCK)))
    return jnp.swapaxes(out, 0, 1).reshape(B_, S_, H, Dh)

def hybrid_layer(h, p_i, rel_bias, norm_mix, w_in, qn_a, kn_a, qn_c, kn_c, w_alpha2, b_alpha,
                 gla_norm, w_out_a, w_out_b, w_out_c, w_gate, b_gate, w_o, norm_ffn,
                 w_ffn_gate, w_ffn_up, w_ffn_down, norm_ple, w_ple_gate, w_ple_proj):
    B_, S_, _ = h.shape
    dt = h.dtype
    u = rms_norm(h, norm_mix)
    parts = jnp.split(u @ w_in, _IN_OFFSETS, axis=-1)
    a_q, a_k, a_v, b_q, b_k, b_v, b_r, b_al, c_q, c_k, c_v, i_q, i_k, i_w = parts

    def heads(t, nh):
        return t.reshape(B_, S_, nh, -1)

    qa = rms_norm(heads(a_q, DSWA_HEADS), qn_a) * HEAD_DIM ** -0.5
    ka = rms_norm(heads(a_k, DSWA_HEADS), kn_a)
    o_a = mixer_dilated(qa, ka, heads(a_v, DSWA_HEADS), rel_bias[:, :DSWA_HEADS])
    y_a = o_a.reshape(B_, S_, -1).astype(dt) @ w_out_a
    o_b = mixer_gla(heads(b_q, GLA_HEADS), heads(b_k, GLA_HEADS), heads(b_v, GLA_HEADS), b_al, w_alpha2, b_alpha)
    o_b = rms_norm(o_b, gla_norm) * jax.nn.silu(heads(b_r, GLA_HEADS).astype(jnp.float32))
    y_b = o_b.reshape(B_, S_, -1).astype(dt) @ w_out_b
    qc = rms_norm(heads(c_q, DSA_HEADS), qn_c) * HEAD_DIM ** -0.5
    kc = rms_norm(c_k, kn_c)
    o_c = mixer_dsa(qc, kc, c_v, heads(i_q, IDX_HEADS), i_k, i_w, rel_bias[:, DSWA_HEADS:])
    y_c = o_c.reshape(B_, S_, -1).astype(dt) @ w_out_c
    g_a, g_b, g_c = jnp.split(jax.nn.sigmoid(u @ w_gate + b_gate), 3, axis=-1)
    h = h + (g_a * y_a + g_b * y_b + g_c * y_c) @ w_o
    f = rms_norm(h, norm_ffn)
    h = h + (jax.nn.silu(f @ w_ffn_gate) * (f @ w_ffn_up)) @ w_ffn_down
    e = rms_norm(h, norm_ple)
    h = h + jax.nn.sigmoid(e @ w_ple_gate) * (p_i @ w_ple_proj)
    return h

def setup_inputs(seed: int = 0) -> dict:
    key = jax.random.key(seed)
    ks = iter(jax.random.split(key, 32))

    def nrm(shape, scale):
        return jax.random.normal(next(ks), shape, jnp.float32) * scale

    def gain(shape):
        return 1.0 + nrm(shape, 0.05)

    D = D_MODEL
    return {
        "x": nrm((BATCH, SEQ, D), 1.0),
        "p": nrm((DEPTH, BATCH, SEQ, PLE_DIM), 1.0),
        "rel_bias": nrm((REL_BUCKETS, N_BIAS_HEADS), 0.2),
        "norm_mix": gain((DEPTH, D)),
        "w_in": nrm((DEPTH, D, N_IN), D ** -0.5),
        "qn_a": gain((DEPTH, HEAD_DIM)),
        "kn_a": gain((DEPTH, HEAD_DIM)),
        "qn_c": gain((DEPTH, HEAD_DIM)),
        "kn_c": gain((DEPTH, HEAD_DIM)),
        "w_alpha2": nrm((DEPTH, GLA_GATE_RANK, GLA_HEADS * GLA_DK), GLA_GATE_RANK ** -0.5),
        "b_alpha": nrm((DEPTH, GLA_HEADS * GLA_DK), 0.1),
        "gla_norm": gain((DEPTH, GLA_DV)),
        "w_out_a": nrm((DEPTH, DSWA_HEADS_PER_GROUP * HEAD_DIM, D), (DSWA_HEADS_PER_GROUP * HEAD_DIM) ** -0.5),
        "w_out_b": nrm((DEPTH, GLA_HEADS * GLA_DV, D), (GLA_HEADS * GLA_DV) ** -0.5),
        "w_out_c": nrm((DEPTH, DSA_HEADS * HEAD_DIM, D), (DSA_HEADS * HEAD_DIM) ** -0.5),
        "w_gate": nrm((DEPTH, D, 3 * D), D ** -0.5),
        "b_gate": nrm((DEPTH, 3 * D), 0.1),
        "w_o": nrm((DEPTH, D, D), D ** -0.5),
        "norm_ffn": gain((DEPTH, D)),
        "w_ffn_gate": nrm((DEPTH, D, D_FF), D ** -0.5),
        "w_ffn_up": nrm((DEPTH, D, D_FF), D ** -0.5),
        "w_ffn_down": nrm((DEPTH, D_FF, D), D_FF ** -0.5),
        "norm_ple": gain((DEPTH, D)),
        "w_ple_gate": nrm((DEPTH, D, D), D ** -0.5),
        "w_ple_proj": nrm((DEPTH, PLE_DIM, D), PLE_DIM ** -0.5),
    }

def reference(x, p, rel_bias, norm_mix, w_in, qn_a, kn_a, qn_c, kn_c, w_alpha2, b_alpha, gla_norm,
              w_out_a, w_out_b, w_out_c, w_gate, b_gate, w_o, norm_ffn, w_ffn_gate, w_ffn_up,
              w_ffn_down, norm_ple, w_ple_gate, w_ple_proj):
    h = x
    for i in range(DEPTH):
        h = hybrid_layer(h, p[i], rel_bias, norm_mix[i], w_in[i], qn_a[i], kn_a[i], qn_c[i], kn_c[i],
                         w_alpha2[i], b_alpha[i], gla_norm[i], w_out_a[i], w_out_b[i], w_out_c[i],
                         w_gate[i], b_gate[i], w_o[i], norm_ffn[i], w_ffn_gate[i], w_ffn_up[i],
                         w_ffn_down[i], norm_ple[i], w_ple_gate[i], w_ple_proj[i])
    return h


_drawn_inputs = setup_inputs


def setup_inputs(seed=0):
    import zlib

    import numpy as np

    out = dict(_drawn_inputs(seed))
    spreads = {}
    factors = {'qn_a': 8.0,
     'kn_a': 8.0,
     'qn_c': 8.0,
     'kn_c': 8.0,
     'b_alpha': 3.862,
     'gla_norm': 3.583,
     'b_gate': 4.271,
     'norm_ple': 22.812,
     'rel_bias': 4.822}
    for name, (base, spread) in spreads.items():
        noise = np.random.default_rng([zlib.crc32(name.encode()), seed]).standard_normal(out[name].shape)
        drawn = base * np.exp(spread * noise) if base else spread * noise
        out[name] = __import__('jax').numpy.asarray(drawn.astype(out[name].dtype))
    for name, factor in factors.items():
        out[name] = (out[name] * factor).astype(out[name].dtype)
    return out
```

```python
from contextlib import ExitStack

import numpy as np

import concourse.bass as bass
from concourse import mybir

F32 = mybir.dt.float32
F32R = mybir.dt.float32r
ALU = mybir.AluOpType
ACT = mybir.ActivationFunctionType

P = 128
S = 512
D = 1024
KD = D // P
NT = S // P
HD = 64
EPS = 1e-6
A_SLOTS, A_GROUPS = 4, 3
C_HEADS = 12
IDX_HEADS = 8
TOPK = 128
GH, GV, CH = 4, 256, 64
NCH = S // CH
TAU = 16.0
FF = 2816
KF = FF // P
PLE = 256
CW = 256
BUCKETS, MAX_DIST = 32, 2048
RV = S + P
DILATIONS = ((128, 1), (512, 4), (2048, 16))
NEG = -1.0e30
HIDDEN = -3.0e38
TAKEN = -3.4e38
_W = (768, 768, 768, 512, 512, 1024, 1024, 16, 768, 64, 64, 512, 64, 8)
(O_AQ, O_AK, O_AV, O_BQ, O_BK, O_BV, O_BR, O_AL, O_CQ, O_CK, O_CV, O_IQ, O_IK, O_IW) = (
    sum(_W[:i]) for i in range(len(_W)))


def shape_tables():
    dist = np.arange(RV) - (P - 1)
    d = np.maximum(dist, 0)
    exact = BUCKETS // 2
    large = exact + (np.log(np.maximum(d, 1).astype(np.float32) / np.float32(exact))
                     / np.float32(np.log(MAX_DIST / exact)) * np.float32(BUCKETS - exact)).astype(np.int32)
    bucket = np.where(d < exact, d, np.minimum(large, BUCKETS - 1))
    onehot = np.zeros((BUCKETS, RV), np.float32)
    onehot[bucket, np.arange(RV)] = 1.0
    mask = np.zeros((24, RV), np.float32)
    mask[:, dist < 0] = NEG
    for g, (window, dilation) in enumerate(DILATIONS):
        mask[4 * g:4 * g + 4, (dist % dilation != 0) | (dist > window)] = NEG
    p, f = np.arange(P)[:, None], np.arange(P)[None, :]
    ident = (p == f).astype(np.float32)
    head_ones = (p // HD == f // HD).astype(np.float32)
    hidden = np.where(f > p, np.float32(HIDDEN), np.float32(0))
    chunk_causal = ((f >= p) & (p // CH == f // CH)).astype(np.float32)
    return onehot, mask, np.concatenate([ident, head_ones, hidden, chunk_causal, np.ones((P, P), np.float32)], 1)


def build(nc, t, out):
    ctx = ExitStack()
    with ctx:
        base = (nc.sbuf_base + 63) // 64 * 64
        place = [base]

        def sb(name, shape, dt, at=None):
            size = int(np.prod(shape[1:])) * 4
            if at is None:
                at = place[0]
                place[0] += (size + 31) // 32 * 32
            return nc.alloc_sbuf_tensor_at(name, shape, dt, offset=at)

        TB = 4 * S
        w_raw = [sb(f"w_raw{i}", [P, KD * CW], F32) for i in range(2)]
        w_hi = [sb(f"w_hi{i}", [P, KD * CW], F32R) for i in range(2)]
        w_lo = [sb(f"w_lo{i}", [P, KD * CW], F32R) for i in range(2)]
        hT = sb("hT", [P, KD, S], F32)
        u_hi = sb("u_hi", [P, KD, S], F32R)
        u_lo = sb("u_lo", [P, KD, S], F32R)
        region = place[0]
        s_hi = sb("s_hi", [P, KF, S], F32R)
        s_lo = sb("s_lo", [P, KF, S], F32R)
        place[0] += 10 * TB
        tables = sb("tables", [P, 5 * P], F32)
        ident, head_ones, hidden = (tables[:, i * P:(i + 1) * P] for i in range(3))
        chunk_causal, ones = tables[:, 3 * P:4 * P], tables[:, 4 * P:5 * P]
        vec = sb("vec", [P, 58], F32)
        gains, bg = vec[:, 0:24].rearrange("p (n k) -> p n k", n=3), vec[:, 24:48]
        ba, gg, head_gains = vec[:, 48:52], vec[:, 52:54], vec[:, 54:58]
        iw = sb("iw", [P, NT, 8], F32)
        st = sb("st", [P, 64], F32)
        token_root = st[:, 44:48]
        top8 = sb("top8", [P, 3, 8], F32)
        wa2_sb = sb("wa2_sb", [P, P], F32)
        decay = sb("decay", [P, NCH], F32)
        assert place[0] <= nc.sbuf_usable_end, (place[0], nc.sbuf_usable_end)

        def tile(name, i, n=1, shape=None):
            return nc.alloc_sbuf_tensor_at(name, shape or [P, int(n * S)], F32, offset=region + i * TB)

        x_in_sb = [tile(f"x_in_sb{t_}", 24 + 2 * t_, 2) for t_ in range(NT)]
        onehot_sb, mask_sb, rv_sb = tile("onehot_sb", 8, 2), tile("mask_sb", 10, 2), tile("rv_sb", 50, 2)
        relb_sb, vec_rows = tile("relb_sb", 12), tile("vec_rows", 13)
        sq = [tile("sq0", 44), tile("sq1", 45)]
        sq_sum, rstd = tile("sq_sum", 46), tile("rstd", 47)
        normed = [tile("normed0", 48), tile("normed1", 49)]
        qa = [tile(f"qa{i}", 2 + i) for i in range(6)]
        ka = [tile(f"ka{i}", 24 + i) for i in range(6)]
        va = tile("va", 44, 6, [P, NT, 768])
        cq = [tile(f"cq{i}", 16 + i) for i in range(6)]
        iq = [tile(f"iq{i}", 38 + i) for i in range(4)]
        ck, ik = tile("ck", 42), tile("ik", 43)
        cv = nc.alloc_sbuf_tensor_at("cv", [P, NT, HD], F32, offset=region + 37 * TB + TB // 2)
        al = tile("al", 31)
        head_tmp = tile("head_tmp", 53)
        bqk = [tile(f"bqk{i}", 44 + i) for i in range(8)]
        bv = [tile(f"bv{i}", (24, 26, 28, 6)[i], 2) for i in range(NT)]
        sa = [tile("sa0", 50, 3), tile("sa1", 8, 3)]
        pta = [tile("pta0", 32, 3), tile("pta1", 35, 2.5)]
        bias_a = [[tile(f"bias_a{r}{g}", (11, 12, 13, 14, 15, 30)[3 * r + g]) for g in range(3)] for r in range(2)]
        sc = [tile("sc0", 52), tile("sc1", 53)]
        ptc = [tile("ptc0", 38), tile("ptc1", 39)]
        bias_c = [tile(f"bias_c{i}", (5, 9, 30, 43)[i]) for i in range(4)]
        score = [None, tile("score1", 2), tile("score2", 3), tile("score3", 4)]
        relu = [tile("relu0", 52), tile("relu1", 53)]
        g_t = [tile(f"g_t{i}", (2, 3, 4, 5, 20, 21)[i]) for i in range(6)]
        g_state = [tile(f"g_state{i}", 16 + i, 1, [P, 2, GV]) for i in range(4)]
        g_reset = tile("g_reset", 9)
        part = [tile(f"part{d}", 38 + d if d < 6 else 46 + d) for d in range(KD)]
        gate_t = [tile("gate_t0", 8), tile("gate_t1", 30)]
        silu_r = [tile(f"silu_r{i}", 16 + i) for i in range(4)]
        gate_b_t = [tile(f"gate_b_t{i}", 44 + i) for i in range(4)]
        silu_g = [tile("silu_g0", 44), tile("silu_g1", 45)]
        prod = [tile("prod0", 46, 1, [P, 1, S]), tile("prod1", 48, 1, [P, 1, S])]
        sq_row = [tile(f"sq_row{c}", 44 + c, 1, [P, 1, S]) for c in range(2)]
        normed_row = [tile(f"normed_row{c}", 48 + c, 1, [P, 1, S]) for c in range(2)]
        p_sb = tile("p_sb", 50, 2, [P, NT, PLE])
        p_hi, p_lo = (nc.alloc_sbuf_tensor_at(n_, [P, 2, S], F32R, offset=region + i * TB)
                      for n_, i in (("p_hi_sb", 50), ("p_lo_sb", 52)))
        pp = [tile(f"pp{t_}", 2 + 2 * t_, 2) for t_ in range(NT)]
        sig = [tile("sig0", 12, 1, [P, 2, CW]), tile("sig1", 13, 1, [P, 2, CW])]
        out_sb = [tile(f"out_sb{i}", 14 + i, 1, [P, 2, CW]) for i in range(8)]

        merged = [(s_hi[:, i, :], s_lo[:, i, :]) for i in (10, 11, 12, 13, 14, 15, 0, 1)]

        bank = [ctx.enter_context(nc.psum_tensor(f"bank{i}", [P, S], F32)) for i in range(8)]
        QK, TR, OUT, MISC = (2, 3), (4, 5), 6, 7

        names = """const_in x_in_all bias_vec_out xt_done xt_free sq_done sum_done ss_done rstd_done normed_done
            u_hi_done u_lo_done hi_ready lo_ready w_used proj_done head_raw head_sq head_ss head_rstd head_normed
            rv_mm rv_done qk_done s_ready exp_done p_ready t_done t_free pv_done o_hi_done o_lo_done relu_done
            relu_used sel_done v_done b_done gl_L gl_abs gl_min gl_ln gl_scan gl_e gl_qk gl_tk gl_kend gl_att
            gl_attT gl_u gl_state gl_o gl_osq gl_ss gl_r gl_out e_done sig_ready part_done r_done r_prod r_hi r_lo
            m_sum m_hi m_lo h2_done ff_silu ff_scaled ff_hi ff_lo h3_done p_in pt_done p_hi p_lo pp_done
            ple_sig ple_mul ht_done out_ready out_done dve_step act_step hg_in hg_done small_done index_in
            reset_done scratch_done wa2_in vec_turned vec_done""".split()
        sem = {n: ctx.enter_context(nc.semaphore(n)) for n in names}
        raw_in = [ctx.enter_context(nc.semaphore(f"raw_in{i}")) for i in range(2)]
        proj_free = [ctx.enter_context(nc.semaphore(f"proj_free{i}")) for i in range(4)]
        qk_free = [ctx.enter_context(nc.semaphore(f"qk_free{i}")) for i in range(2)]
        x_in = [ctx.enter_context(nc.semaphore(f"x_in{i}")) for i in range(NT)]
        bias_a_in = [ctx.enter_context(nc.semaphore(f"bias_a_in{i}")) for i in range(2)]
        bias_c_in = [ctx.enter_context(nc.semaphore(f"bias_c_in{i}")) for i in range(4)]

        def rows(name):
            return t[name][0].rearrange("(k p) n -> p k n", p=P)

        w_in = rows("w_in")

        def cols(w, c0, n=CW):
            return w[:, :, c0:c0 + n]

        slots, groups, g_of = [], [], {}

        def slot(kc, width, loads):
            slots.append((kc, width, loads))
            return len(slots) - 1

        def group(key, n, kind, x=None, c0=0, m=P, kc=KD, toks=None, nc_=None):
            g_of[key] = len(groups)
            groups.append(dict(slot=n, kind=kind, x=x, c0=c0, m=m, kc=kc, toks=toks, n=nc_))

        def u_tile(k):
            return u_hi[:, k, :], u_lo[:, k, :]

        def o_tile(i):
            return s_hi[:, i, :], s_lo[:, i, :]

        def feature_slots(key, w, c0, count, kc=KD, x=u_tile):
            for i in range(count):
                n = slot(kc, CW, [(0, cols(w, c0 + CW * i))])
                for c in range(2):
                    group((key, 2 * i + c), n, "feat", x, P * c, P, kc)

        def token_slots(key, w, c0, count):
            for i in range(count):
                n = slot(KD, CW, [(0, cols(w, c0 + CW * i))])
                for c in range(2):
                    group((key, 2 * i + c), n, "tok", u_tile, 0, toks=(2 * c, 2 * c + 1), nc_=CW)

        feature_slots("aq", w_in, O_AQ, 3)
        feature_slots("ak", w_in, O_AK, 3)
        token_slots("av", w_in, O_AV, 3)
        T1_GROUPS = len(groups)
        n_ = slot(KD, 88, [(0, cols(w_in, O_AL, 16)), (16, cols(w_in, O_CV, HD)), (80, cols(w_in, O_IW, 8))])
        group(("cviw", 0), n_, "tok", u_tile, 16, toks=(0, 1, 2, 3), nc_=72)
        group(("al", 0), n_, "feat", u_tile, 0, 88)
        feature_slots("iq", w_in, O_IQ, 2)
        n_ = slot(KD, CW, [(HD * i, cols(w_in, (O_CK, O_CK, O_IK, O_IK)[i], HD)) for i in range(4)])
        group(("ck", 0), n_, "feat", u_tile, 0)
        group(("ik", 0), n_, "feat", u_tile, P)
        feature_slots("cq", w_in, O_CQ, 3)
        T2_GROUPS = len(groups)
        feature_slots("bq", w_in, O_BQ, 2)
        feature_slots("bk", w_in, O_BK, 2)
        token_slots("bv", w_in, O_BV, 4)
        T3_GROUPS = len(groups)
        w_gate = rows("w_gate")
        feature_slots("ga", w_gate, 0, 4)
        n_ = slot(2, D, [(0, rows("w_out_a"))])
        for d_ in range(KD):
            group(("ya", d_), n_, "feat", lambda k: o_tile(k), P * d_, P, 2)
        w_oc, w_ob, w_oo = rows("w_out_c"), rows("w_out_b"), rows("w_o")
        for j_ in range(4):
            for key, w, kc, x in (("gc", w_gate, KD, u_tile), ("yc", w_oc, 6, lambda k: o_tile(10 + k))):
                n_ = slot(kc, CW, [(0, cols(w, (2 * D if key == "gc" else 0) + CW * j_))])
                for c in range(2):
                    group((key, 2 * j_ + c), n_, "feat", x, P * c, P, kc)
        T4_GROUPS = len(groups)
        feature_slots("br", w_in, O_BR, 4)
        for j_ in range(4):
            for key, w, x in (("gb", w_gate, u_tile), ("yb", w_ob, lambda k: o_tile(2 + k))):
                n_ = slot(KD, CW, [(0, cols(w, (D if key == "gb" else 0) + CW * j_))])
                for c in range(2):
                    group((key, 2 * j_ + c), n_, "feat", x, P * c, P, KD)
        feature_slots("wo", w_oo, 0, 4, x=lambda k: merged[k])
        PRE_SLOTS, PRE_GROUPS = len(slots), len(groups)
        assert PRE_SLOTS % 2 == 1

        kind_of = {g: key for key, g in g_of.items()}
        last_group = {}
        uses, bank_of, use_of = [0] * 4, [], []
        for g, gr in enumerate(groups):
            b_ = g % 2 if g < T4_GROUPS else g % 4
            bank_of.append(b_)
            use_of.append(uses[b_])
            if kind_of[g][0] != "wo":
                uses[b_] += 1
            last_group[gr["slot"]] = g
        first_group = {}
        for g, gr in enumerate(groups):
            first_group.setdefault(gr["slot"], g)
        landed, total_ = [], [0, 0]
        for n, (_, _, loads) in enumerate(slots):
            total_[n % 2] += len(loads)
            landed.append(total_[n % 2])

        FFN_N, DOWN_N = PRE_SLOTS, PRE_SLOTS + 2 * (FF // CW)
        DOWN_ROWS = ((0, 6), (6, 6), (12, 5), (17, 5))
        PLE_N = DOWN_N + 4 * (D // CW)
        FFN_G, DOWN_G = PRE_GROUPS, PRE_GROUPS + 4 * (FF // CW)
        PLE_G = DOWN_G + 2 * (D // CW)
        FI, DI = FF // CW, D // CW

        def landed_value(n, i=0):
            if n < PRE_SLOTS:
                return 16 * landed[n]
            return 16 * (total_[n % 2] + (n - PRE_SLOTS) // 2 + 1) + 16 * i

        def raw_view(n, kc, width):
            return w_raw[n % 2][:, 0:kc * width].rearrange("p (k c) -> p k c", k=kc)

        def part_views(n, kc, width):
            return (w_hi[n % 2][:, 0:kc * width].rearrange("p (k c) -> p k c", k=kc),
                    w_lo[n % 2][:, 0:kc * width].rearrange("p (k c) -> p k c", k=kc))

        def wait_slot_used(eng, n):
            if n >= 0:
                eng.wait_ge(sem["proj_done"], last_group[n] + 1)

        units, n_qk, n_tr, n_ready = [], 0, 0, 0
        for u in range(64):
            if u < 16:
                s_, b = u // 4, u % 4
                half = s_ % 2
                kb0 = [max(b - 1, 0), 0, 0]
                subs, blocks, at = [], [], 0
                for g in range(A_GROUPS):
                    hd_ = 4 * g + s_
                    k0, k1 = kb0[g], b + 1
                    subs.append(dict(q=qa[hd_ // 2], k=ka[hd_ // 2], k0=k0 * P, k1=k1 * P, at=at,
                                     bias=bias_a[s_ % 2][g]))
                    for kb in range(k0, k1):
                        blocks.append((at + (kb - k0) * P, va[:, kb, HD * hd_:HD * hd_ + HD]))
                    at += (k1 - k0) * P
                S_, PT_ = sa[u % 2], pta[u % 2]
            else:
                h, b = (u - 16) // 4, (u - 16) % 4
                half = h % 2
                subs = [dict(q=cq[h // 2], k=ck, k0=0, k1=(b + 1) * P, at=0, bias=bias_c[h % 4])]
                blocks = [(kb * P, cv[:, kb, :]) for kb in range(b + 1)]
                at = (b + 1) * P
                S_, PT_ = sc[u % 2], ptc[u % 2]
            if u == 16:
                n_qk += 3 * IDX_HEADS
            chunks = [blocks[i:i + 4] for i in range(0, len(blocks), 4)]
            units.append(dict(b=b, half=half, subs=subs, chunks=chunks, width=at, S=S_, PT=PT_, qk0=n_qk,
                              tr0=n_tr))
            if u >= 16 and b == 0:
                units[-1]["ready"] = (qk_free[n_qk % 2], n_qk // 2 + 1)
            else:
                n_ready += 1
                units[-1]["ready"] = (sem["s_ready"], n_ready)
            n_qk += len(subs)
            n_tr += len(chunks)
        IDX_QK0 = 48
        idx = [(b, h) for b in (1, 2, 3) for h in range(IDX_HEADS)]
        pair_tile = [0, 1, 10, 11, 12, 13, 14, 15]

        def ple_free(g):
            return uses[g % 4] + FI + g // 4

        chains = ([(g_of["aq", i], qa[i], 0) for i in range(6)] + [(g_of["ak", i], ka[i], 1) for i in range(6)]
                  + [(g_of["ck", 0], ck, 3)] + [(g_of["cq", i], cq[i], 2) for i in range(6)])
        chain_at = {c[0]: i for i, c in enumerate(chains)}

        STEPS = 5 * GH
        t4 = list(range(T3_GROUPS, T4_GROUPS))
        t4_step = [t4[j * len(t4) // STEPS:(j + 1) * len(t4) // STEPS] for j in range(STEPS)]

        CONSTS = 16 * 18
        st_ = lambda u, i: st[:, (u % 4) * 8 + i:(u % 4) * 8 + i + 1]

        block = ctx.enter_context(nc.Block())

        @block.sync
        def _(sp):
            def load(n):
                kc, width, loads = slots[n]
                if n >= 2:
                    sp.wait_ge(sem["hi_ready"], n - 1)
                    sp.wait_ge(sem["lo_ready"], n - 1)
                for c0, src in loads:
                    sp.dma_start(raw_view(n, kc, width)[:, :, c0:c0 + src.shape[2]], src).then_inc(raw_in[n % 2], 16)

            x_v = t["x"][0].rearrange("(t p) d -> t p d", p=P)
            for tb in range(NT):
                sp.dma_start(x_in_sb[tb][:, :], x_v[tb]).then_inc(x_in[tb], 16)
            for n in range(PRE_SLOTS):
                load(n)

            w_fg, w_fu, w_fd = rows("w_ffn_gate"), rows("w_ffn_up"), rows("w_ffn_down")
            with sp.Fori(0, FI) as i:
                for c, w in enumerate((w_fg, w_fu)):
                    sp.wait_ge(sem["hi_ready"], i * 2 + (FFN_N + c - 1))
                    sp.wait_ge(sem["lo_ready"], i * 2 + (FFN_N + c - 1))
                    sp.dma_start(raw_view(FFN_N + c, KD, CW), w[:, :, bass.ds(i * CW, CW)]).then_inc(
                        raw_in[(FFN_N + c) % 2], 16)
            with sp.Fori(0, DI) as i:
                for c, (k0, kc) in enumerate(DOWN_ROWS):
                    sp.wait_ge(sem["hi_ready"], i * 4 + (DOWN_N + c - 1))
                    sp.wait_ge(sem["lo_ready"], i * 4 + (DOWN_N + c - 1))
                    sp.dma_start(raw_view(DOWN_N + c, kc, CW), w_fd[:, k0:k0 + kc, bass.ds(i * CW, CW)]).then_inc(
                        raw_in[(DOWN_N + c) % 2], 16)
            w_pp, w_pg = rows("w_ple_proj"), rows("w_ple_gate")
            for j in range(5):
                n = PLE_N + j
                sp.wait_ge(sem["hi_ready"], n - 1)
                sp.wait_ge(sem["lo_ready"], n - 1)
                if j == 0:
                    sp.dma_start(raw_view(n, 2, D), w_pp).then_inc(raw_in[n % 2], 16)
                else:
                    sp.dma_start(raw_view(n, KD, CW), cols(w_pg, CW * (j - 1))).then_inc(raw_in[n % 2], 16)
            out_v = out[0].rearrange("(t p) d -> p t d", p=P)
            for i in range(8):
                j, tp = i // 2, i % 2
                sp.wait_ge(sem["out_ready"], i + 1)
                sp.dma_start(out_v[:, 2 * tp:2 * tp + 2, CW * j:CW * j + CW], out_sb[i][:, :, :]).then_inc(
                    sem["out_done"], 16)
            sp.wait_ge(sem["out_done"], 8 * 16)

        @block.gpsimd
        def _(pool):
            def lo(n, kc, width, i2=0):
                pool.wait_ge(sem["hi_ready"], i2 + (n + 1))
                r = slice(0, kc * width)
                pool.tensor_tensor(w_lo[n % 2][:, r], w_raw[n % 2][:, r], w_hi[n % 2][:, r].bitcast(F32),
                                   ALU.subtract).then_inc(sem["lo_ready"], 1)

            for n in range(PRE_SLOTS):
                wait_slot_used(pool, n - 2)
                lo(n, slots[n][0], slots[n][1])
            with pool.Fori(0, FI) as i:
                for c in range(2):
                    lo(FFN_N + c, KD, CW, i * 2)
            with pool.Fori(0, DI) as i:
                for c, (_, kc) in enumerate(DOWN_ROWS):
                    lo(DOWN_N + c, kc, CW, i * 4)
            for j in range(5):
                lo(PLE_N + j, *((2, D) if j == 0 else (KD, CW)))

        @block.scalar
        def _(act):
            own = [0]

            def link(ins):
                own[0] += 1
                ins.then_inc(sem["act_step"], 1)
                act.wait_ge(sem["act_step"], own[0])

            def hi(n, kc=None, width=None, i_landed=0):
                if kc is None:
                    kc, width = slots[n][:2]
                act.wait_ge(raw_in[n % 2], landed_value(n) + i_landed)
                r = slice(0, kc * width)
                act.copy(w_hi[n % 2][:, r], w_raw[n % 2][:, r]).then_inc(sem["hi_ready"], 1)

            def next_hi(g):
                n = groups[g]["slot"]
                if first_group[n] == g:
                    if n + 1 < PRE_SLOTS:
                        wait_slot_used(act, n - 1)
                        hi(n + 1)
                    else:
                        wait_slot_used(act, n - 1)
                        hi(FFN_N, KD, CW)

            def dma(dst, src, s=None):
                act.dma_start(dst, src).then_inc(sem["const_in"] if s is None else s, 16)

            nc.scalar.preload_act_table_set("natural_log_exp_and_others")
            dma(tables[:, :], t["c_tables"])
            dma(relb_sb[0:BUCKETS, 0:24], t["rel_bias"])
            dma(onehot_sb[0:BUCKETS, 0:RV], t["c_onehot"])
            dma(mask_sb[0:24, 0:RV], t["c_mask"])
            for i, name in enumerate(("norm_mix", "norm_ffn", "norm_ple")):
                dma(vec_rows[8 * i:8 * i + 8, 0:P], t[name][0].rearrange("(k p) -> k p", p=P))
            for i, name in enumerate(("qn_a", "kn_a", "qn_c", "kn_c")):
                for half in range(2):
                    dma(vec_rows[54 + i:55 + i, HD * half:HD * half + HD], t[name])
            dma(vec_rows[24:48, 0:P], t["b_gate"][0].rearrange("(k p) -> k p", p=P))
            dma(vec_rows[48:52, 0:P], t["b_alpha"][0].rearrange("(k p) -> k p", p=P))
            dma(wa2_sb[0:16, :], t["w_alpha2"][0, :, 0:P], sem["wa2_in"])
            dma(vec_rows[52:54, 0:P], t["gla_norm"][0].rearrange("(k p) -> k p", p=P))

            def root(j, dst, total):
                act.wait_ge(sem["ss_done"], j + 1)
                link(act.activation(dst, total, ACT.Ln, scale=1.0 / D, bias=st[:, 40:41]))
                act.activation(dst, dst, ACT.Exp, scale=-0.5).then_inc(sem["rstd_done"], 1)

            def norm(j):
                for d in range(KD):
                    if d >= 2:
                        act.wait_ge(sem["sum_done"], KD * j + d - 1)
                    act.wait_ge(sem["h2_done"], KD * j + d + 1)
                    act.activation(sq[d % 2][:, :], hT[:, d, :], ACT.Square).then_inc(sem["sq_done"], 1)
                act.wait_ge(sem["small_done"], 1)
                root(j, rstd[:, :], bank[MISC][:, :])
                for d in range(KD):
                    act.wait_ge(sem["normed_done"], KD * j + d + 1)
                    act.copy(u_hi[:, d, :], normed[d % 2][:, :]).then_inc(sem["u_hi_done"], 1)

            norm(0)
            hi(0)

            def load_bias(dst, head, s):
                src = t["c_scratch"]
                act.dma_start(dst[:, :], bass.AP(tensor=src.tensor, offset=head * RV, ap=[[1, P], [1, S]])).then_inc(s, 16)

            act.wait_ge(sem["rv_done"], 2)
            act.dma_start(t["c_scratch"], rv_sb[0:24, 0:RV]).then_inc(sem["scratch_done"], 16)
            act.wait_ge(sem["scratch_done"], 16)

            def load_bias_a(s_):
                for g in range(A_GROUPS):
                    load_bias(bias_a[s_ % 2][g], 4 * g + s_, bias_a_in[s_ % 2])

            load_bias_a(0)
            load_bias_a(1)

            def head_norm(g):
                if g - 1 in chain_at:
                    c = chain_at[g - 1]
                    act.wait_ge(sem["head_ss"], c + 1)
                    link(act.activation(head_tmp[:, :], bank[MISC][:, :], ACT.Ln, scale=1.0 / HD, bias=st[:, 40:41]))
                    act.activation(head_tmp[:, :], head_tmp[:, :], ACT.Exp, scale=-0.5).then_inc(sem["head_rstd"], 1)
                if g in chain_at:
                    c = chain_at[g]
                    act.wait_ge(proj_free[bank_of[g]], use_of[g] + 1)
                    if c:
                        act.wait_ge(sem["head_normed"], c)
                    act.activation(head_tmp[:, :], chains[c][1][:, :], ACT.Square).then_inc(sem["head_sq"], 1)

            def take_bank(g, dst, src=None):
                act.wait_ge(sem["proj_done"], g + 1)
                act.copy(dst, bank[bank_of[g]][:, :] if src is None else src).then_inc(proj_free[bank_of[g]], 1)

            def tok_view(g, w=CW):
                return bank[bank_of[g]][:, 0:2 * w].rearrange("p (t c) -> p t c", t=2)

            for g in range(T1_GROUPS):
                next_hi(g)
                head_norm(g)
                if kind_of[g][0] == "av":
                    i, c = kind_of[g][1] // 2, kind_of[g][1] % 2
                    take_bank(g, va[:, 2 * c:2 * c + 2, CW * i:CW * i + CW], tok_view(g))

            def exp(u):
                U = units[u]
                act.wait_ge(*U["ready"])
                act.activation(U["S"][:, 0:U["width"]], U["S"][:, 0:U["width"]], ACT.Exp, bias=st_(u, 3), scale=-1.0,
                               accum_out=st_(u, 4)).then_inc(sem["exp_done"], 1)

            def take_probs(u):
                U = units[u]
                if u >= 2:
                    act.wait_ge(sem["pv_done"], u - 1)
                for c, ch in enumerate(U["chunks"]):
                    k = U["tr0"] + c
                    act.wait_ge(sem["t_done"], k + 1)
                    w = P * len(ch)
                    act.copy(U["PT"][:, 4 * P * c:4 * P * c + w], bank[TR[k % 2]][:, 0:w]).then_inc(sem["t_free"], 1)

            def out_hi(u):
                if u % 8 == 7:
                    act.wait_ge(sem["pv_done"], u + 1)
                    act.copy(s_hi[:, pair_tile[u // 8], :], bank[OUT][:, :]).then_inc(sem["o_hi_done"], 1)

            for i in range(18):
                if i < 16:
                    exp(i)
                    if i % 4 == 3 and i // 4 + 2 < A_SLOTS:
                        load_bias_a(i // 4 + 2)
                g = T1_GROUPS + i
                if g < T2_GROUPS:
                    next_hi(g)
                if g <= T2_GROUPS:
                    head_norm(g)
                if 1 <= i <= 16:
                    take_probs(i - 1)
                if i >= 2:
                    out_hi(i - 2)

            def take_b(g):
                next_hi(g)
                key, i = kind_of[g]
                if key in ("bq", "bk"):
                    take_bank(g, bqk[2 * i + (key == "bk")][:, :])
                else:
                    j, c = i // 2, i % 2
                    act.wait_ge(sem["proj_done"], g + 1)
                    act.copy(bv[2 * c][:, CW * j:CW * j + CW], bank[bank_of[g]][:, 0:CW])
                    act.copy(bv[2 * c + 1][:, CW * j:CW * j + CW], bank[bank_of[g]][:, CW:2 * CW]).then_inc(
                        proj_free[bank_of[g]], 1)

            act.wait_ge(sem["pv_done"], 16)
            for e, (b, h) in enumerate(idx):
                k = IDX_QK0 + e
                act.wait_ge(sem["qk_done"], k + 1)
                if e >= 2:
                    act.wait_ge(sem["relu_used"], e - 1)
                w = P * (b + 1)
                act.activation(relu[e % 2][:, 0:w], bank[QK[k % 2]][:, 0:w], ACT.Relu).then_inc(qk_free[k % 2], 1)
                if e % 6 == 5:
                    take_b(T2_GROUPS + e // 6)
            act.wait_ge(sem["relu_used"], 24)
            for h in range(4):
                load_bias(bias_c[h], C_HEADS + h, bias_c_in[h])
            for g in range(T2_GROUPS + 4, T2_GROUPS + 11):
                take_b(g)
            for j in range(50):
                if j < 48:
                    exp(16 + j)
                    if j % 4 == 3 and j // 4 + 4 < C_HEADS:
                        h = j // 4 + 4
                        load_bias(bias_c[h % 4], C_HEADS + h, bias_c_in[h % 4])
                if j % 2 == 0 and j < 10:
                    take_b(T2_GROUPS + 11 + j // 2)
                if 1 <= j <= 48:
                    take_probs(16 + j - 1)
                if j >= 2:
                    out_hi(16 + j - 2)

            def gla(h, stage):
                if stage == 0:
                    act.wait_ge(sem["gl_L"], h + 1)
                    if h:
                        act.wait_ge(sem["gl_ss"], h)
                    act.activation(g_t[0][:, :], bank[2][:, :], ACT.Abs, bias=ba[:, h:h + 1]).then_inc(sem["gl_abs"], 1)
                    act.wait_ge(sem["gl_abs"], h + 1)
                    link(act.activation(g_t[0][:, :], g_t[0][:, :], ACT.Exp, scale=-1.0))
                    act.activation(g_t[0][:, :], g_t[0][:, :], ACT.Ln, bias=st[:, 41:42]).then_inc(sem["gl_ln"], 1)
                    act.wait_ge(sem["gl_scan"], h + 1)
                    cum = g_t[2]
                    act.activation(g_t[3][:, :], cum[:, :], ACT.Exp, scale=1.0 / TAU).then_inc(sem["gl_e"], 1)
                    act.activation(g_t[4][:, :], cum[:, :], ACT.Exp, scale=-1.0 / TAU).then_inc(sem["gl_e"], 1)
                    act.activation(g_t[1][:, :], g_t[0][:, :], ACT.Exp, scale=1.0 / TAU).then_inc(sem["gl_e"], 1)
                    if h:
                        act.wait_ge(sem["gl_state"], (NCH - 1) * h)
                    act.activation(decay[:, :], cum[:, CH - 1:S:CH], ACT.Exp, scale=1.0 / TAU).then_inc(sem["gl_e"], 1)
                    if h + 1 < GH:
                        dma(wa2_sb[0:16, :], t["w_alpha2"][0, :, P * (h + 1):P * (h + 2)], sem["wa2_in"])
                elif stage == 1:
                    act.wait_ge(sem["gl_tk"], h + 1)
                    act.copy(g_t[1][:, :], bank[2][:, :]).then_inc(sem["gl_kend"], 1)
                elif stage == 3:
                    for e in range(2):
                        act.wait_ge(sem["gl_o"], 2 * h + e + 1)
                        act.copy(g_t[4 + e][:, :], bank[(OUT, MISC)[e]][:, :]).then_inc(sem["gl_osq"], 1)
                        act.wait_ge(sem["gl_osq"], 4 * h + 2 * e + 1)
                        act.activation(g_t[e][:, :], g_t[4 + e][:, :], ACT.Square).then_inc(sem["gl_osq"], 1)
                elif stage == 4:
                    act.wait_ge(sem["gl_ss"], h + 1)
                    link(act.activation(g_t[2][:, :], bank[2][:, :], ACT.Ln, scale=1.0 / GV, bias=st[:, 40:41]))
                    act.activation(g_t[2][:, :], g_t[2][:, :], ACT.Exp, scale=-0.5).then_inc(sem["gl_r"], 1)

            def gate_exp(g):
                key, d = kind_of[g]
                if key not in ("ga", "gc", "br", "gb"):
                    return
                dst, bias = {"ga": lambda: (part[d], bg[:, d:d + 1]),
                             "gc": lambda: (gate_t[d % 2], bg[:, 16 + d:17 + d]),
                             "br": lambda: (silu_r[d % 4], 0.0),
                             "gb": lambda: (gate_b_t[d % 4], bg[:, 8 + d:9 + d])}[key]()
                if key == "gc" and d >= 2:
                    act.wait_ge(sem["part_done"], d - 1)
                if key == "br" and d >= 4:
                    act.wait_ge(sem["r_lo"], d - 3)
                if key == "gb" and d == 0:
                    act.wait_ge(sem["r_lo"], KD)
                if key == "gb" and d >= 4:
                    act.wait_ge(sem["m_lo"], d - 3)
                act.wait_ge(sem["proj_done"], g + 1)
                act.activation(dst[:, :], bank[bank_of[g]][:, :], ACT.Exp, scale=-1.0, bias=bias).then_inc(
                    sem["r_done"] if key == "br" else proj_free[bank_of[g]], 1)

            act.wait_ge(sem["pv_done"], 64)
            act.wait_ge(sem["o_lo_done"], 8)
            for j in range(STEPS):
                gla(j // 5, j % 5)
                for g in t4_step[j]:
                    next_hi(g)
                    gate_exp(g)

            for g in range(T4_GROUPS, g_of["wo", 0]):
                next_hi(g)
                if kind_of[g][0] == "gb" and kind_of[g][1] == 0:
                    act.wait_ge(sem["r_prod"], KD)
                    act.copy(s_hi[:, 2 + KD - 1, :], silu_r[(KD - 1) % 4][:, :]).then_inc(sem["r_hi"], 1)
                gate_exp(g)
                key, d = kind_of[g]
                if key == "br" and d >= 1:
                    act.wait_ge(sem["r_prod"], d)
                    act.copy(s_hi[:, 2 + d - 1, :], silu_r[(d - 1) % 4][:, :]).then_inc(sem["r_hi"], 1)
                if key == "yb":
                    act.wait_ge(sem["m_sum"], d + 1)
                    act.copy(merged[d][0], gate_b_t[d % 4][:, :]).then_inc(sem["m_hi"], 1)
            dma(p_sb[:, :, :], t["p"][0, 0].rearrange("(t p) c -> p t c", p=P), sem["p_in"])

            for d in range(KD):
                next_hi(g_of["wo", d])
                act.wait_ge(sem["normed_done"], KD + d + 1)
                act.copy(u_hi[:, d, :], normed[d % 2][:, :]).then_inc(sem["u_hi_done"], 1)
                if d == KD - 1:
                    act.wait_ge(sem["proj_done"], FFN_G)
                    hi(FFN_N + 1, KD, CW)
                if d >= 2:
                    act.wait_ge(sem["sum_done"], KD + d - 1)
                act.activation(sq[d % 2][:, :], hT[:, d, :], ACT.Square).then_inc(sem["sq_done"], 1)
            root(1, rstd[:, :], bank[MISC][:, :])

            def ffn(i, first=False, last=False):
                if not first:
                    act.wait_ge(sem["proj_done"], i * 4 + FFN_G)
                    hi(FFN_N + 1, KD, CW, i * 16)
                for c in range(2):
                    act.wait_ge(proj_free[c], i + (uses[c] + 1))
                    act.activation(silu_g[c][:, :], silu_g[c][:, :], ACT.Silu).then_inc(sem["ff_silu"], 1)
                act.wait_ge(sem["proj_done"], i * 4 + (FFN_G + 2))
                if last:
                    hi(DOWN_N, DOWN_ROWS[0][1], CW)
                else:
                    hi(FFN_N, KD, CW, (i + 1) * 16)
                for c in range(2):
                    act.wait_ge(proj_free[2 + c], i + (uses[2 + c] + 1))
                    act.copy(s_hi[:, bass.ds(i * 2 + c, 1), :], prod[c][:, :, :]).then_inc(sem["ff_hi"], 1)

            ffn(0, first=True)
            with act.Fori(1, FI - 1) as i:
                ffn(i)
            ffn(FI - 1, last=True)

            for k in range(2):
                act.wait_ge(sem["pt_done"], 2)
                act.copy(p_hi[:, k, :], bank[TR[k]][:, :]).then_inc(sem["p_hi"], 1)

            def rows_hi(i):
                for c in range(2):
                    act.wait_ge(sem["normed_done"], i * 2 + (2 * KD + c + 1))
                    act.copy(u_hi[:, bass.ds(i * 2 + c, 1), :], normed_row[c][:, :, :]).then_inc(
                        sem["u_hi_done"], 1)
                    act.wait_ge(sem["sum_done"], i * 2 + (2 * KD + c - 1))
                    act.activation(sq_row[c][:, :, :], hT[:, bass.ds(i * 2 + c, 1), :], ACT.Square).then_inc(
                        sem["sq_done"], 1)

            def down(i, first=False, last=False):
                for c in range(4):
                    if c == 0:
                        act.wait_ge(sem["proj_done"], i * 2 + DOWN_G)
                    else:
                        act.wait_ge(sem["w_used"], i * 3 + c)
                    if c < 3:
                        hi(DOWN_N + c + 1, DOWN_ROWS[c + 1][1], CW, i * 32)
                        if c == 1 and not first:
                            rows_hi(i - 1)
                    elif last:
                        hi(PLE_N, 2, D)
                    else:
                        hi(DOWN_N, DOWN_ROWS[0][1], CW, (i + 1) * 32)

            down(0, first=True)
            with act.Fori(1, DI - 1) as i:
                down(i)
            down(DI - 1, last=True)

            rows_hi(DI - 1)
            act.wait_ge(sem["proj_done"], PLE_G)
            hi(PLE_N + 1, KD, CW)
            for g in range(8):
                tb, c = g // 2, g % 2
                act.wait_ge(sem["proj_done"], PLE_G + g + 1)
                act.copy(pp[tb][:, S * c:S * c + S], bank[g % 4][:, :]).then_inc(proj_free[g % 4], 1)
            root(2, token_root, bank[MISC][:, 0:NT])
            act.wait_ge(sem["rstd_done"], 3)
            for j in range(4):
                if j < 3:
                    act.wait_ge(sem["proj_done"], PLE_G + 8 + 2 * j)
                    hi(PLE_N + 2 + j, KD, CW)
                for c in range(2):
                    q = 2 * j + c
                    act.wait_ge(sem["proj_done"], PLE_G + 8 + q + 1)
                    if q >= 2:
                        act.wait_ge(sem["out_ready"], q - 1)
                    for i in range(2):
                        ins = act.activation(sig[q % 2][:, i, :], bank[q % 4][:, CW * i:CW * i + CW], ACT.Sigmoid,
                                             scale=token_root[:, 2 * c + i:2 * c + i + 1])
                    ins.then_inc(proj_free[q % 4], 1)

        @block.vector
        def _(dve):
            own = [0]

            def link(ins):
                own[0] += 1
                ins.then_inc(sem["dve_step"], 1)
                dve.wait_ge(sem["dve_step"], own[0])

            dve.memset(st[:, 40:41], EPS)
            dve.memset(st[:, 41:42], 1.0).then_inc(sem["small_done"], 1)

            def norm_sum(j, d):
                dve.wait_ge(sem["sq_done"], KD * j + d + 1)
                if d == 0:
                    ins = dve.tensor_copy(sq_sum[:, :], sq[0][:, :])
                else:
                    dve.wait_ge(sem["sum_done"], KD * j + d)
                    ins = dve.tensor_tensor(sq_sum[:, :], sq_sum[:, :], sq[d % 2][:, :], ALU.add)
                ins.then_inc(sem["sum_done"], 1)

            def norm_scale(j):
                dve.wait_ge(sem["rstd_done"], j + 1)

                def lo(d):
                    dve.wait_ge(sem["u_hi_done"], KD * j + d + 1)
                    dve.tensor_tensor(u_lo[:, d, :], normed[d % 2][:, :], u_hi[:, d, :].bitcast(F32),
                                      ALU.subtract).then_inc(sem["u_lo_done"], 1)

                for d in range(KD):
                    if d >= 2:
                        lo(d - 2)
                        dve.wait_ge(sem["u_lo_done"], KD * j + d - 1)
                    dve.scalar_tensor_tensor(normed[d % 2][:, :], hT[:, d, :], gains[:, j, d:d + 1], rstd[:, :],
                                             ALU.mult, ALU.mult).then_inc(sem["normed_done"], 1)
                lo(KD - 2)
                lo(KD - 1)

            for d in range(KD):
                dve.wait_ge(sem["xt_done"], d + 1)
                dve.tensor_copy(hT[:, d, :], bank[QK[d % 2]][:, :]).then_inc(sem["h2_done"], 1)
                if d >= 1:
                    norm_sum(0, d - 1)
            norm_sum(0, KD - 1)
            dve.wait_ge(sem["const_in"], CONSTS)
            dve.wait_ge(sem["rv_mm"], 2)
            dve.tensor_tensor(rv_sb[0:24, 0:S], bank[TR[0]][0:24, :], mask_sb[0:24, 0:S], ALU.add).then_inc(
                sem["rv_done"], 1)
            dve.tensor_tensor(rv_sb[0:24, S:RV], bank[TR[1]][0:24, 0:P], mask_sb[0:24, S:RV], ALU.add).then_inc(
                sem["rv_done"], 1)
            dve.wait_ge(sem["vec_turned"], 1)
            link(dve.tensor_copy(vec[:, :], bank[OUT][:, 0:58]))
            for i in (54, 56):
                link(dve.tensor_scalar(vec[:, i:i + 1], vec[:, i:i + 1], HD ** -0.5, None, ALU.mult))
            dve.tensor_scalar(bg, bg, -1.0, None, ALU.mult).then_inc(sem["vec_done"], 1)
            dve.wait_ge(sem["vec_done"], 1)
            norm_scale(0)

            def head_raw(g):
                if g in chain_at:
                    dve.wait_ge(sem["proj_done"], g + 1)
                    dve.tensor_copy(chains[chain_at[g]][1][:, :], bank[bank_of[g]][:, :]).then_inc(
                        proj_free[bank_of[g]], 1)
                if g - 1 in chain_at:
                    c = chain_at[g - 1]
                    dst = chains[c][1]
                    dve.wait_ge(sem["head_rstd"], c + 1)
                    dve.scalar_tensor_tensor(dst[:, :], dst[:, :], head_gains[:, chains[c][2]:chains[c][2] + 1],
                                             head_tmp[:, :], ALU.mult, ALU.mult).then_inc(sem["head_normed"], 1)

            for g in range(T1_GROUPS):
                head_raw(g)

            def scores(u):
                U = units[u]
                n = len(U["subs"])
                if u >= 2 and u not in (16, 17):
                    V = units[u - 2]
                    dve.wait_ge(sem["t_done"], V["tr0"] + len(V["chunks"]))
                if u < 16:
                    if U["b"] == 0:
                        dve.wait_ge(bias_a_in[u // 4 % 2], 48 * (u // 8 + 1))
                elif U["b"] == 0:
                    h = (u - 16) // 4
                    dve.wait_ge(bias_c_in[h % 4], 16 * (h // 4 + 1))
                for g, sub in enumerate(U["subs"]):
                    k, w = U["qk0"] + g, sub["k1"] - sub["k0"]
                    first = P * (U["b"] + 1) - 1 - sub["k0"]
                    seg, full = U["S"][:, sub["at"]:sub["at"] + w], sub["bias"][:, :]
                    table = bass.AP(tensor=full.tensor, offset=full.offset + first, ap=[[S, P], [-1, w]])
                    dve.wait_ge(sem["qk_done"], k + 1)
                    if u >= 16 and U["b"] > 0:
                        dve.tensor_tensor(seg, bank[QK[k % 2]][:, 0:w], table, ALU.add).then_inc(qk_free[k % 2], 1)
                        dve.wait_ge(qk_free[k % 2], k // 2 + 1)
                        ins = dve.tensor_tensor_reduce(seg, seg, score[U["b"]][:, 0:w], -1.0, 3.0e38, ALU.add,
                                                       ALU.min, st_(u, 3))
                        ins.then_inc(sem["s_ready"], 1)
                    elif u >= 16:
                        ins = dve.tensor_tensor_reduce(seg, bank[QK[k % 2]][:, 0:w], table, -1.0, 3.0e38, ALU.add,
                                                       ALU.min, st_(u, 3))
                        ins.then_inc(qk_free[k % 2], 1)
                    else:
                        ins = dve.tensor_tensor_reduce(seg, bank[QK[k % 2]][:, 0:w], table, -1.0, 3.0e38, ALU.add,
                                                       ALU.min, st_(u, g))
                        ins.then_inc(qk_free[k % 2], 1)
                        if g == n - 1:
                            for q in (k - 1, k):
                                dve.wait_ge(qk_free[q % 2], q // 2 + 1)
                            dve.tensor_reduce(st_(u, 3), st[:, (u % 4) * 8:(u % 4) * 8 + 3],
                                              mybir.AxisListType.X, ALU.min).then_inc(sem["s_ready"], 1)

            def normalise(u):
                U = units[u]
                dve.wait_ge(sem["exp_done"], u + 1)
                link(dve.reciprocal(st_(u, 5), st_(u, 4)))
                dve.tensor_scalar(U["S"][:, 0:U["width"]], U["S"][:, 0:U["width"]], st_(u, 5), None,
                                  ALU.mult).then_inc(sem["p_ready"], 1)

            def out_lo(u):
                if u % 8 == 7:
                    i = pair_tile[u // 8]
                    dve.wait_ge(sem["o_hi_done"], u // 8 + 1)
                    dve.tensor_tensor(s_lo[:, i, :], bank[OUT][:, :], s_hi[:, i, :].bitcast(F32),
                                      ALU.subtract).then_inc(sem["o_lo_done"], 1)

            for i in range(18):
                if i < 16:
                    scores(i)
                g = T1_GROUPS + i
                if g < T2_GROUPS:
                    key, j = kind_of[g]
                    b_ = bank_of[g]
                    if key in ("iq", "ik", "al"):
                        dst = iq[j] if key == "iq" else ik if key == "ik" else al
                        r = slice(0, 16 if key == "al" else P)
                        dve.wait_ge(sem["proj_done"], g + 1)
                        dve.tensor_copy(dst[r, :], bank[b_][r, :]).then_inc(proj_free[b_], 1)
                    if key == "cviw":
                        v = bank[b_][:, 0:288].rearrange("p (t c) -> p t c", t=NT)
                        dve.wait_ge(sem["proj_done"], g + 1)
                        dve.tensor_copy(cv[:, :, :], v[:, :, 0:HD])
                        dve.tensor_scalar(iw[:, :, :], v[:, :, HD:HD + 8], IDX_HEADS ** -0.5 * HD ** -0.5, None,
                                          ALU.mult).then_inc(proj_free[b_], 1)
                if g <= T2_GROUPS:
                    head_raw(g)
                if 1 <= i <= 16:
                    normalise(i - 1)
                if i >= 2:
                    out_lo(i - 2)

            for e, (b, h) in enumerate(idx):
                w = P * (b + 1)
                dve.wait_ge(sem["qk_done"], IDX_QK0 + e + 1)
                dve.wait_ge(qk_free[(IDX_QK0 + e) % 2], (IDX_QK0 + e) // 2 + 1)
                if e:
                    dve.wait_ge(sem["relu_used"], e)
                if h == 0:
                    ins = dve.tensor_scalar(score[b][:, 0:w], relu[e % 2][:, 0:w], iw[:, b, h:h + 1], None, ALU.mult)
                else:
                    ins = dve.scalar_tensor_tensor(score[b][:, 0:w], relu[e % 2][:, 0:w], iw[:, b, h:h + 1],
                                                   score[b][:, 0:w], ALU.mult, ALU.add)
                ins.then_inc(sem["relu_used"], 1)
            dve.wait_ge(sem["relu_used"], 24)
            steps = [0]

            def topk_step(ins, b):
                ins.then_inc(sem["index_in"], 1)
                steps[0] += 1
                done[b] = steps[0]

            done = {}
            for b in (1, 2, 3):
                topk_step(dve.tensor_tensor(score[b][:, P * b:P * b + P], score[b][:, P * b:P * b + P], hidden,
                                            ALU.add), b)
            for r in range(TOPK // 8):
                for b in (1, 2, 3):
                    dve.wait_ge(sem["index_in"], done[b])
                    topk_step(dve.max(top8[:, b - 1, :], score[b][:, 0:P * (b + 1)]), b)
                for b in (1, 2, 3):
                    dve.wait_ge(sem["index_in"], done[b])
                    topk_step(dve.match_replace(score[b][:, 0:P * (b + 1)], top8[:, b - 1, :],
                                                score[b][:, 0:P * (b + 1)], TAKEN), b)
            for b in (1, 2, 3):
                dve.wait_ge(sem["index_in"], done[b])
                link(dve.tensor_scalar(score[b][:, 0:P * (b + 1)], score[b][:, 0:P * (b + 1)],
                                       (HIDDEN + TAKEN) / 2, NEG, ALU.is_gt, ALU.mult))

            for j in range(50):
                if j < 48:
                    scores(16 + j)
                if 1 <= j <= 48:
                    normalise(16 + j - 1)
                if j >= 2:
                    out_lo(16 + j - 2)

            link(dve.memset(g_reset[:, :], 1.0))
            dve.memset(g_reset[:, 0:S:CH], 0.0).then_inc(sem["reset_done"], 1)
            dve.wait_ge(sem["reset_done"], 1)

            def gla(h, stage):
                if stage == 0:
                    lf, cum = g_t[1], g_t[2]
                    dve.wait_ge(sem["gl_abs"], h + 1)
                    link(dve.tensor_scalar(lf[:, :], bank[2][:, :], ba[:, h:h + 1], 0.0, ALU.add, ALU.min))
                    dve.wait_ge(sem["gl_ln"], h + 1)
                    link(dve.tensor_tensor(lf[:, :], lf[:, :], g_t[0][:, :], ALU.subtract))
                    dve.tensor_tensor_scan(cum[:, :], g_reset[:, :], lf[:, :], 0.0, ALU.mult, ALU.add).then_inc(
                        sem["gl_min"], 1)
                    dve.wait_ge(sem["gl_min"], h + 1)
                    last = cum[:, CH - 1:S:CH]
                    dve.tensor_tensor(g_t[0][:, :].rearrange("p (n c) -> p n c", c=CH),
                                      last.unsqueeze(2).to_broadcast([P, NCH, CH]),
                                      cum[:, :].rearrange("p (n c) -> p n c", c=CH), ALU.subtract).then_inc(
                        sem["gl_scan"], 1)
                    dve.wait_ge(sem["gl_e"], 4 * h + 1)
                    dve.scalar_tensor_tensor(bqk[2 * h][:, :], bqk[2 * h][:, :], float(P) ** -0.5, g_t[3][:, :],
                                             ALU.mult, ALU.mult).then_inc(sem["gl_qk"], 1)
                    dve.wait_ge(sem["gl_e"], 4 * h + 2)
                    dve.tensor_tensor(g_t[5][:, :], bqk[2 * h + 1][:, :], g_t[4][:, :], ALU.mult).then_inc(
                        sem["gl_qk"], 1)
                    dve.wait_ge(sem["gl_e"], 4 * h + 3)
                    dve.tensor_tensor(bqk[2 * h + 1][:, :], bqk[2 * h + 1][:, :], g_t[1][:, :], ALU.mult).then_inc(
                        sem["gl_qk"], 1)
                elif stage == 1:
                    dve.wait_ge(sem["gl_att"], h + 1)
                    dve.tensor_tensor(g_t[3][:, :].rearrange("p (n c) -> p n c", c=P),
                                      bank[3][:, :].rearrange("p (n c) -> p n c", c=P),
                                      chunk_causal.unsqueeze(1).to_broadcast([P, NT, P]), ALU.mult).then_inc(
                        sem["gl_attT"], 1)
                elif stage == 2:
                    dve.wait_ge(sem["gl_e"], 4 * h + 4)
                    for c in range(NCH - 1):
                        dst = g_state[c // 2][:, c % 2, :]
                        src = bank[TR[c % 2]][:, 0:GV]
                        dve.wait_ge(sem["gl_u"], (NCH - 1) * h + c + 1)
                        if c == 0:
                            ins = dve.tensor_copy(dst, src)
                        else:
                            ins = dve.scalar_tensor_tensor(dst, g_state[(c - 1) // 2][:, (c - 1) % 2, :],
                                                           decay[:, c:c + 1], src, ALU.mult, ALU.add)
                        ins.then_inc(sem["gl_state"], 1)
                        dve.wait_ge(sem["gl_state"], (NCH - 1) * h + c + 1)
                elif stage == 4:
                    dve.wait_ge(sem["gl_r"], h + 1)
                    for e in range(2):
                        dve.scalar_tensor_tensor(bqk[2 * h + e][:, :], g_t[4 + e][:, :], gg[:, e:e + 1],
                                                 g_t[2][:, :], ALU.mult, ALU.mult).then_inc(sem["gl_out"], 1)

            def gate(g):
                key, d = kind_of[g]
                b_ = bank_of[g]
                if key in ("ga", "gc", "gb"):
                    dst = {"ga": lambda: part[d], "gc": lambda: gate_t[d % 2], "gb": lambda: gate_b_t[d % 4]}[key]()
                    dve.wait_ge(proj_free[b_], use_of[g] + 1)
                    link(dve.tensor_scalar(dst[:, :], dst[:, :], 1.0, None, ALU.add))
                    link(dve.reciprocal(dst[:, :], dst[:, :]))
                elif key == "ya":
                    dve.wait_ge(sem["proj_done"], g + 1)
                    dve.tensor_tensor(part[d][:, :], part[d][:, :], bank[b_][:, :], ALU.mult).then_inc(
                        proj_free[b_], 1)
                    dve.wait_ge(proj_free[b_], use_of[g] + 1)
                elif key == "yc":
                    dve.wait_ge(sem["proj_done"], g + 1)
                    dve.tensor_tensor(gate_t[d % 2][:, :], gate_t[d % 2][:, :], bank[b_][:, :], ALU.mult).then_inc(
                        proj_free[b_], 1)
                    dve.wait_ge(proj_free[b_], use_of[g] + 1)
                    dve.tensor_tensor(part[d][:, :], part[d][:, :], gate_t[d % 2][:, :], ALU.add).then_inc(
                        sem["part_done"], 1)
                elif key == "br":
                    tmp = silu_r[d % 4]
                    dve.wait_ge(sem["r_done"], d + 1)
                    link(dve.tensor_scalar(tmp[:, :], tmp[:, :], 1.0, None, ALU.add))
                    link(dve.reciprocal(tmp[:, :], tmp[:, :]))
                    dve.tensor_tensor(tmp[:, :], tmp[:, :], bank[b_][:, :], ALU.mult).then_inc(proj_free[b_], 1)
                    dve.wait_ge(proj_free[b_], use_of[g] + 1)
                    dve.tensor_tensor(tmp[:, :], tmp[:, :], bqk[d][:, :], ALU.mult).then_inc(sem["r_prod"], 1)
                elif key == "yb":
                    tmp = gate_b_t[d % 4]
                    dve.wait_ge(sem["proj_done"], g + 1)
                    dve.tensor_tensor(tmp[:, :], tmp[:, :], bank[b_][:, :], ALU.mult).then_inc(proj_free[b_], 1)
                    dve.wait_ge(proj_free[b_], use_of[g] + 1)
                    dve.tensor_tensor(tmp[:, :], tmp[:, :], part[d][:, :], ALU.add).then_inc(sem["m_sum"], 1)

            for j in range(STEPS):
                gla(j // 5, j % 5)
                for g in t4_step[j]:
                    gate(g)

            def r_lo(d):
                dve.wait_ge(sem["r_hi"], d + 1)
                dve.tensor_tensor(s_lo[:, 2 + d, :], silu_r[d % 4][:, :], s_hi[:, 2 + d, :].bitcast(F32),
                                  ALU.subtract).then_inc(sem["r_lo"], 1)

            def m_lo(d):
                dve.wait_ge(sem["m_hi"], d + 1)
                dve.tensor_tensor(merged[d][1], gate_b_t[d % 4][:, :], merged[d][0].bitcast(F32),
                                  ALU.subtract).then_inc(sem["m_lo"], 1)

            for g in range(T4_GROUPS, g_of["wo", 0]):
                key, d = kind_of[g]
                if key == "gb" and d == 0:
                    r_lo(KD - 1)
                gate(g)
                if key == "br" and d >= 1:
                    r_lo(d - 1)
                if key == "yb":
                    m_lo(d)
            for d in range(KD):
                g = g_of["wo", d]
                dve.wait_ge(sem["proj_done"], g + 1)
                dve.tensor_tensor(hT[:, d, :], hT[:, d, :], bank[bank_of[g]][:, :], ALU.add).then_inc(
                    sem["h2_done"], 1)
                dve.wait_ge(sem["h2_done"], KD + d + 1)
                if d >= 2:
                    dve.wait_ge(sem["u_lo_done"], KD + d - 1)
                dve.tensor_scalar(normed[d % 2][:, :], hT[:, d, :], gains[:, 1, d:d + 1], None,
                                  ALU.mult).then_inc(sem["normed_done"], 1)
                if d:
                    norm_sum(1, d - 1)
                dve.wait_ge(sem["u_hi_done"], KD + d + 1)
                dve.tensor_tensor(u_lo[:, d, :], normed[d % 2][:, :], u_hi[:, d, :].bitcast(F32),
                                  ALU.subtract).then_inc(sem["u_lo_done"], 1)
            norm_sum(1, KD - 1)
            dve.wait_ge(sem["rstd_done"], 2)

            def ffn(i, first=False):
                for c in range(2):
                    dve.wait_ge(sem["proj_done"], i * 4 + (FFN_G + 1 + c))
                    if not first:
                        dve.wait_ge(proj_free[2 + c], i + uses[2 + c])
                    dve.tensor_tensor(silu_g[c][:, :], bank[c][:, :], rstd[:, :], ALU.mult).then_inc(proj_free[c], 1)
                for c in range(2):
                    dve.wait_ge(sem["ff_silu"], i * 2 + (c + 1))
                    dve.tensor_tensor(silu_g[c][:, :], silu_g[c][:, :], rstd[:, :], ALU.mult).then_inc(
                        sem["ff_scaled"], 1)
                if not first:
                    dve.wait_ge(sem["ff_lo"], i * 2)
                def lo(c):
                    dve.wait_ge(sem["ff_hi"], i * 2 + (c + 1))
                    dve.tensor_tensor(s_lo[:, bass.ds(i * 2 + c, 1), :], prod[c][:, :, :],
                                      s_hi[:, bass.ds(i * 2 + c, 1), :].bitcast(F32),
                                      ALU.subtract).then_inc(sem["ff_lo"], 1)

                for c in range(2):
                    dve.wait_ge(sem["proj_done"], i * 4 + (FFN_G + 3 + c))
                    dve.wait_ge(sem["ff_scaled"], i * 2 + (c + 1))
                    dve.tensor_tensor(prod[c][:, 0, :], silu_g[c][:, :], bank[2 + c][:, :], ALU.mult).then_inc(
                        proj_free[2 + c], 1)
                for c in range(2):
                    lo(c)

            ffn(0, first=True)
            with dve.Fori(1, FI) as i:
                ffn(i)

            for k in range(2):
                dve.wait_ge(sem["p_hi"], k + 1)
                dve.tensor_tensor(p_lo[:, k, :], bank[TR[k]][:, :], p_hi[:, k, :].bitcast(F32),
                                  ALU.subtract).then_inc(sem["p_lo"], 1)

            dve.wait_ge(sem["ff_lo"], KF)
            link(dve.memset(sq_sum[:, :], 0.0))
            with dve.Fori(0, DI) as i:
                for c in range(2):
                    dve.wait_ge(sem["proj_done"], i * 2 + (DOWN_G + c + 1))
                    row = hT[:, bass.ds(i * 2 + c, 1), :]
                    dve.tensor_tensor(row, row, bank[c][:, :].unsqueeze(1), ALU.add).then_inc(sem["h2_done"], 1)
                    dve.wait_ge(sem["h2_done"], i * 2 + (2 * KD + c + 1))
                    dve.wait_ge(sem["u_lo_done"], i * 2 + (2 * KD + c - 1))
                    dve.tensor_tensor(normed_row[c][:, :, :], row,
                                      gains[:, 2, bass.ds(i * 2 + c, 1)].unsqueeze(2).to_broadcast([P, 1, S]),
                                      ALU.mult).then_inc(sem["normed_done"], 1)
                for c in range(2):
                    dve.wait_ge(sem["u_hi_done"], i * 2 + (2 * KD + c + 1))
                    dve.tensor_tensor(u_lo[:, bass.ds(i * 2 + c, 1), :], normed_row[c][:, :, :],
                                      u_hi[:, bass.ds(i * 2 + c, 1), :].bitcast(F32),
                                      ALU.subtract).then_inc(sem["u_lo_done"], 1)
                    dve.wait_ge(sem["sq_done"], i * 2 + (2 * KD + c + 1))
                    dve.wait_ge(sem["sum_done"], i * 2 + (2 * KD + c))
                    dve.tensor_tensor(sq_sum[:, :], sq_sum[:, :], sq_row[c][:, 0, :], ALU.add).then_inc(
                        sem["sum_done"], 1)

            for j in range(4):
                for c in range(2):
                    q = 2 * j + c
                    dve.wait_ge(proj_free[q % 4], ple_free(8 + q) + 1)
                    sg = sig[q % 2]
                    for i in range(2):
                        ins = dve.tensor_tensor(sg[:, i, :], sg[:, i, :], pp[2 * c + i][:, CW * j:CW * j + CW],
                                                ALU.mult)
                    link(ins)
                    dve.wait_ge(sem["ht_done"], q + 1)
                    dve.tensor_tensor(out_sb[q][:, :, :], sg[:, :, :],
                                      bank[TR[q % 2]][:, :].rearrange("p (t c) -> p t c", t=2),
                                      ALU.add).then_inc(sem["out_ready"], 1)

        @block.tensor
        def _(pe):
            def mm3(dst, w, x, start, stop):
                (wh, wl), (xh, xl) = w, x
                pe.matmul(dst, wh, xh, start=start, stop=False)
                pe.matmul(dst, wh, xl, start=False, stop=False)
                return pe.matmul(dst, wl, xh, start=False, stop=stop)

            def project(g):
                G = groups[g]
                n, b_ = G["slot"], bank_of[g]
                kc, width, _ = slots[n]
                wh, wl = part_views(n, kc, width)
                if first_group[n] == g:
                    pe.wait_ge(sem["lo_ready"], n + 1)
                if use_of[g]:
                    pe.wait_ge(proj_free[b_], use_of[g])
                if kind_of[g][0] == "wo" and kind_of[g][1] >= 4:
                    pe.wait_ge(sem["h2_done"], KD + kind_of[g][1] - 3)
                if G["kind"] == "feat":
                    c = slice(G["c0"], G["c0"] + G["m"])
                    for k in range(kc):
                        last = mm3(bank[b_][0:G["m"], :], (wh[:, k, c], wl[:, k, c]), G["x"](k), k == 0, k == kc - 1)
                else:
                    w = G["n"]
                    c = slice(G["c0"], G["c0"] + w)
                    for i, tb in enumerate(G["toks"]):
                        r = slice(P * tb, P * tb + P)
                        for k in range(kc):
                            last = mm3(bank[b_][:, w * i:w * i + w], (u_hi[:, k, r], u_lo[:, k, r]),
                                       (wh[:, k, c], wl[:, k, c]), k == 0, k == kc - 1)
                last.then_inc(sem["proj_done"], 1)

            def norm_total(j):
                pe.wait_ge(sem["sum_done"], KD * (j + 1))
                pe.matmul(bank[MISC][:, :], ones, sq_sum[:, :], start=True, stop=True).then_inc(sem["ss_done"], 1)

            pe.wait_ge(sem["const_in"], CONSTS)
            for h_, (a, b) in enumerate(((0, S), (S, RV))):
                pe.matmul(bank[TR[h_]][0:24, 0:b - a], relb_sb[0:BUCKETS, 0:24], onehot_sb[0:BUCKETS, a:b],
                          start=True, stop=True).then_inc(sem["rv_mm"], 1)
            pe.transpose(bank[OUT][:, 0:58], vec_rows[0:58, 0:P], ident[0:58, 0:58]).then_inc(sem["vec_turned"], 1)
            for d in range(KD):
                if d >= 2:
                    pe.wait_ge(sem["h2_done"], d - 1)
                for tb in range(NT):
                    if d == 0:
                        pe.wait_ge(x_in[tb], 16)
                    last = pe.transpose(bank[QK[d % 2]][:, P * tb:P * tb + P], x_in_sb[tb][:, P * d:P * d + P], ident)
                last.then_inc(sem["xt_done"], 1)
            norm_total(0)
            pe.wait_ge(sem["u_lo_done"], KD)

            def head_sum(g):
                if g in chain_at:
                    c = chain_at[g]
                    pe.wait_ge(sem["head_sq"], c + 1)
                    pe.matmul(bank[MISC][:, :], head_ones, head_tmp[:, :], start=True, stop=True).then_inc(
                        sem["head_ss"], 1)

            for g in range(T1_GROUPS):
                project(g)
                head_sum(g - 1)

            def qk(u):
                U = units[u]
                r = slice(HD * U["half"], HD * U["half"] + HD)
                for g, sub in enumerate(U["subs"]):
                    k = U["qk0"] + g
                    if k >= 2:
                        pe.wait_ge(qk_free[k % 2], k // 2)
                    pe.matmul(bank[QK[k % 2]][:, 0:sub["k1"] - sub["k0"]], sub["q"][r, P * U["b"]:P * U["b"] + P],
                              sub["k"][r, sub["k0"]:sub["k1"]], start=True, stop=True).then_inc(sem["qk_done"], 1)

            def turn(u):
                U = units[u]
                pe.wait_ge(sem["p_ready"], u + 1)
                for c, ch in enumerate(U["chunks"]):
                    k = U["tr0"] + c
                    if k >= 2:
                        pe.wait_ge(sem["t_free"], k - 1)
                    for i, (at, _) in enumerate(ch):
                        last = pe.transpose(bank[TR[k % 2]][:, P * i:P * i + P], U["S"][:, at:at + P], ident)
                    last.then_inc(sem["t_done"], 1)

            def values(u):
                U = units[u]
                pe.wait_ge(sem["t_free"], U["tr0"] + len(U["chunks"]))
                if u % 8 == 0 and u:
                    pe.wait_ge(sem["o_lo_done"], u // 8)
                flat = [v for ch in U["chunks"] for _, v in ch]
                r = slice(HD * U["half"], HD * U["half"] + HD)
                for i, v in enumerate(flat):
                    last = pe.matmul(bank[OUT][r, P * U["b"]:P * U["b"] + P], v, U["PT"][:, P * i:P * i + P],
                                     start=(i == 0), stop=(i == len(flat) - 1))
                last.then_inc(sem["pv_done"], 1)

            pe.wait_ge(sem["head_normed"], 12)
            for i in range(18):
                if i < 16:
                    qk(i)
                if T1_GROUPS + i < T2_GROUPS:
                    project(T1_GROUPS + i)
                if T1_GROUPS + i <= T2_GROUPS:
                    head_sum(T1_GROUPS + i - 1)
                if 1 <= i <= 16:
                    turn(i - 1)
                if i >= 2:
                    values(i - 2)

            for e, (b, h) in enumerate(idx):
                k = IDX_QK0 + e
                r = slice(HD * (h % 2), HD * (h % 2) + HD)
                pe.wait_ge(qk_free[k % 2], k // 2)
                pe.matmul(bank[QK[k % 2]][:, 0:P * (b + 1)], iq[h // 2][r, P * b:P * b + P], ik[r, 0:P * (b + 1)],
                          start=True, stop=True).then_inc(sem["qk_done"], 1)
                if e % 6 == 5:
                    project(T2_GROUPS + e // 6)
            for g in range(T2_GROUPS + 4, T2_GROUPS + 11):
                project(g)
            pe.wait_ge(sem["head_normed"], len(chains))
            qk(16)
            for j in range(50):
                if j + 1 < 48:
                    qk(16 + j + 1)
                if j % 2 == 0 and j < 10:
                    project(T2_GROUPS + 11 + j // 2)
                if 1 <= j <= 48:
                    turn(16 + j - 1)
                if j >= 2:
                    values(16 + j - 2)

            pe.wait_ge(sem["reset_done"], 1)
            pe.wait_ge(sem["o_lo_done"], 8)
            for b_ in range(2):
                pe.wait_ge(proj_free[b_], use_of[T3_GROUPS - 2 + b_] + 1)

            def gla(h, stage):
                if stage == 0:
                    if h:
                        pe.wait_ge(sem["gl_r"], h)
                    pe.wait_ge(sem["wa2_in"], 16 * (h + 1))
                    pe.matmul(bank[2][:, :], wa2_sb[0:16, :], al[0:16, :], start=True,
                              stop=True).then_inc(sem["gl_L"], 1)
                elif stage == 1:
                    pe.wait_ge(sem["gl_qk"], 3 * h + 3)
                    for tb in range(NT):
                        last = pe.transpose(bank[2][:, P * tb:P * tb + P], bqk[2 * h + 1][:, P * tb:P * tb + P], ident)
                    last.then_inc(sem["gl_tk"], 1)
                    for tb in range(NT):
                        r = slice(P * tb, P * tb + P)
                        last = pe.matmul(bank[3][:, r], g_t[5][:, r], bqk[2 * h][:, r], start=True, stop=True)
                    last.then_inc(sem["gl_att"], 1)
                elif stage == 2:
                    pe.wait_ge(sem["gl_kend"], h + 1)
                    for c in range(NCH - 1):
                        q = (NCH - 1) * h + c
                        if q >= 2:
                            pe.wait_ge(sem["gl_state"], q - 1)
                        r = slice(CH * (c % 2), CH * (c % 2) + CH)
                        pe.matmul(bank[TR[c % 2]][:, 0:GV], g_t[1][r, P * (c // 2):P * (c // 2) + P],
                                  bv[c // 2][r, GV * h:GV * h + GV], start=True, stop=True).then_inc(sem["gl_u"], 1)
                elif stage == 3:
                    pe.wait_ge(sem["gl_attT"], h + 1)
                    pe.wait_ge(sem["gl_state"], (NCH - 1) * (h + 1))
                    for e in range(2):
                        b_ = bank[(OUT, MISC)[e]]
                        if h:
                            pe.wait_ge(sem["gl_osq"], 4 * (h - 1) + 2 * e + 1)
                        for tb in range(NT):
                            r = slice(P * tb, P * tb + P)
                            last = pe.matmul(b_[:, r], bv[tb][:, GV * h + P * e:GV * h + P * e + P], g_t[3][:, r],
                                             start=True, stop=False)
                            for c in (2 * tb, 2 * tb + 1):
                                if c:
                                    q = slice(CH * c, CH * c + CH)
                                    last = pe.matmul(b_[:, q], g_state[(c - 1) // 2][:, (c - 1) % 2, P * e:P * e + P],
                                                     bqk[2 * h][:, q], start=False, stop=(c % 2 == 1))
                        last.then_inc(sem["gl_o"], 1)
                else:
                    for e in range(2):
                        pe.wait_ge(sem["gl_osq"], 4 * h + 2 * e + 2)
                        last = pe.matmul(bank[2][:, :], ones, g_t[e][:, :], start=(e == 0), stop=(e == 1))
                    last.then_inc(sem["gl_ss"], 1)

            for j in range(STEPS):
                gla(j // 5, j % 5)
                for g in t4_step[j]:
                    project(g)

            for g in range(T4_GROUPS, PRE_GROUPS):
                key, d = kind_of[g]
                if key == "yb" and d == 0:
                    pe.wait_ge(sem["r_lo"], KD)
                if key == "wo" and d == 0:
                    pe.wait_ge(sem["m_lo"], KD)
                project(g)

            def ffn(i, first=False):
                for half in range(2):
                    n = FFN_N + half
                    wh, wl = part_views(n, KD, CW)
                    pe.wait_ge(sem["lo_ready"], i * 2 + (n + 1))
                    for c in range(2):
                        b_ = 2 * half + c
                        pe.wait_ge(proj_free[b_], i + uses[b_])
                        for k in range(KD):
                            if first and half == 0 and c == 0:
                                pe.wait_ge(sem["u_lo_done"], KD + k + 1)
                            last = mm3(bank[b_][:, :], (wh[:, k, P * c:P * c + P], wl[:, k, P * c:P * c + P]),
                                       u_tile(k), k == 0, k == KD - 1)
                        last.then_inc(sem["proj_done"], 1)
                        if first and half == 0 and c == 0:
                            norm_total(1)

            ffn(0, first=True)
            with pe.Fori(1, FI) as i:
                ffn(i)

            pe.wait_ge(sem["p_in"], 16)
            for k in range(2):
                for tb in range(NT):
                    last = pe.transpose(bank[TR[k]][:, P * tb:P * tb + P], p_sb[:, tb, P * k:P * k + P], ident)
                last.then_inc(sem["pt_done"], 1)

            for b_ in range(4):
                pe.wait_ge(proj_free[b_], uses[b_] + FI)

            def down(i, first=False):
                for j, (k0, kc) in enumerate(DOWN_ROWS):
                    n = DOWN_N + j
                    wh, wl = part_views(n, kc, CW)
                    pe.wait_ge(sem["lo_ready"], i * 4 + (n + 1))
                    for c in range(2):
                        if j == 0:
                            pe.wait_ge(sem["h2_done"], i * 2 + (2 * KD - 1 + c))
                        for k in range(kc):
                            if first and c == 0:
                                pe.wait_ge(sem["ff_lo"], k0 + k + 1)
                            last = mm3(bank[c][:, :], (wh[:, k, P * c:P * c + P], wl[:, k, P * c:P * c + P]),
                                       o_tile(k0 + k), j == 0 and k == 0, j == 3 and k == kc - 1)
                        if j == 3:
                            last.then_inc(sem["proj_done"], 1)
                    if j < 3:
                        last.then_inc(sem["w_used"], 1)

            down(0, first=True)
            with pe.Fori(1, DI) as i:
                down(i)

            pe.wait_ge(sem["p_lo"], 2)
            wh, wl = part_views(PLE_N, 2, D)
            pe.wait_ge(sem["lo_ready"], PLE_N + 1)
            for g in range(8):
                tb, c = g // 2, g % 2
                r, q = slice(P * tb, P * tb + P), slice(S * c, S * c + S)
                if g < 2:
                    pe.wait_ge(sem["h2_done"], 3 * KD - 1 + g)
                pe.wait_ge(proj_free[g % 4], ple_free(g))
                for k in range(2):
                    last = mm3(bank[g % 4][:, :], (p_hi[:, k, r], p_lo[:, k, r]), (wh[:, k, q], wl[:, k, q]),
                               k == 0, k == 1)
                last.then_inc(sem["proj_done"], 1)
            pe.wait_ge(sem["sum_done"], 3 * KD)
            for tb in range(NT):
                last = pe.matmul(bank[MISC][:, tb:tb + 1], sq_sum[:, P * tb:P * tb + P], ones[:, 0:1], start=True,
                                 stop=True)
            last.then_inc(sem["ss_done"], 1)
            pe.wait_ge(sem["u_lo_done"], 3 * KD)
            for j in range(4):
                wh, wl = part_views(PLE_N + 1 + j, KD, CW)
                pe.wait_ge(sem["lo_ready"], PLE_N + 2 + j)
                for c in range(2):
                    q = 2 * j + c
                    pe.wait_ge(proj_free[q % 4], ple_free(8 + q))
                    for i in range(2):
                        r = slice(P * (2 * c + i), P * (2 * c + i) + P)
                        for k in range(KD):
                            last = mm3(bank[q % 4][:, CW * i:CW * i + CW], (u_hi[:, k, r], u_lo[:, k, r]),
                                       (wh[:, k, :], wl[:, k, :]), k == 0, k == KD - 1)
                    last.then_inc(sem["proj_done"], 1)
                    if q >= 2:
                        pe.wait_ge(sem["out_ready"], q - 1)
                    for i in range(2):
                        r = slice(P * (2 * c + i), P * (2 * c + i) + P)
                        for dd in range(2):
                            last = pe.transpose(bank[TR[q % 2]][:, CW * i + P * dd:CW * i + P * dd + P],
                                                hT[:, 2 * j + dd, r], ident)
                    last.then_inc(sem["ht_done"], 1)


_INS = ["x", "p", "rel_bias", "norm_mix", "w_in", "qn_a", "kn_a", "qn_c", "kn_c", "w_alpha2", "b_alpha", "gla_norm",
        "w_out_a", "w_out_b", "w_out_c", "w_gate", "b_gate", "w_o", "norm_ffn", "w_ffn_gate", "w_ffn_up",
        "w_ffn_down", "norm_ple", "w_ple_gate", "w_ple_proj"]


def kernel(**inputs):
    import concourse.bacc as bacc
    from concourse.bass_utils import run_bass_kernel_spmd

    nc = bacc.Bacc("TRN2", target_bir_lowering=False, num_devices=1)
    arrays = {name: np.ascontiguousarray(inputs[name]) for name in _INS}
    arrays["c_onehot"], arrays["c_mask"], arrays["c_tables"] = shape_tables()
    aps = {name: nc.dram_tensor(name, a.shape, mybir.dt.from_np(a.dtype), kind="ExternalInput").ap()
           for name, a in arrays.items()}
    aps["c_scratch"] = nc.dram_tensor("c_scratch", (24, RV), F32, kind="Internal").ap()
    out = nc.dram_tensor("out", (1, S, D), F32, kind="ExternalOutput").ap()
    build(nc, aps, out)
    r = run_bass_kernel_spmd(nc, [arrays], core_ids=[0])
    return r.results[0]["out"]
```

```python
from contextlib import ExitStack

import numpy as np

import concourse.bass as bass
from concourse import mybir

F32 = mybir.dt.float32
F32R = mybir.dt.float32r
ALU = mybir.AluOpType
ACT = mybir.ActivationFunctionType

P = 128
S = 512
D = 1024
KD = D // P
NT = S // P
HD = 64
EPS = 1e-6
A_SLOTS, A_GROUPS = 4, 3
C_HEADS = 12
IDX_HEADS = 8
TOPK = 128
GH, GV, CH = 4, 256, 64
NCH = S // CH
TAU = 16.0
FF = 2816
KF = FF // P
PLE = 256
AVI = 16 + HD + 8
CW = 256
BUCKETS, MAX_DIST = 32, 2048
RV = S + P
DILATIONS = ((128, 1), (512, 4), (2048, 16))
NEG = -1.0e30
HIDDEN = -3.0e38
TAKEN = -3.4e38
T4_SHARE = [7, 2, 3, 3, 2]
LN_EXP = "natural_log_exp_and_others"
_W = (768, 768, 768, 512, 512, 1024, 1024, 16, 768, 64, 64, 512, 64, 8)
(O_AQ, O_AK, O_AV, O_BQ, O_BK, O_BV, O_BR, O_AL, O_CQ, O_CK, O_CV, O_IQ, O_IK, O_IW) = (
    sum(_W[:i]) for i in range(len(_W)))


def shape_tables():
    dist = np.arange(RV) - (P - 1)
    d = np.maximum(dist, 0)
    exact = BUCKETS // 2
    large = exact + (np.log(np.maximum(d, 1).astype(np.float32) / np.float32(exact))
                     / np.float32(np.log(MAX_DIST / exact)) * np.float32(BUCKETS - exact)).astype(np.int32)
    bucket = np.where(d < exact, d, np.minimum(large, BUCKETS - 1))
    onehot = np.zeros((BUCKETS, RV), np.float32)
    onehot[bucket, np.arange(RV)] = 1.0
    mask = np.zeros((24, RV), np.float32)
    mask[:, dist < 0] = NEG
    for g, (window, dilation) in enumerate(DILATIONS):
        mask[4 * g:4 * g + 4, (dist % dilation != 0) | (dist > window)] = NEG
    p, f = np.arange(P)[:, None], np.arange(P)[None, :]
    ident = (p == f).astype(np.float32)
    head_ones = (p // HD == f // HD).astype(np.float32)
    hidden = np.where(f > p, np.float32(HIDDEN), np.float32(0))
    chunk_causal = ((f >= p) & (p // CH == f // CH)).astype(np.float32)
    return onehot, mask, np.concatenate([ident, head_ones, hidden, chunk_causal, np.ones((P, P), np.float32)], 1)


def build(nc, t, out):
    ctx = ExitStack()
    with ctx:
        base = (nc.sbuf_base + 63) // 64 * 64
        place = [base]

        def sb(name, shape, dt, at=None):
            size = int(np.prod(shape[1:])) * 4
            if at is None:
                at = place[0]
                place[0] += (size + 31) // 32 * 32
            return nc.alloc_sbuf_tensor_at(name, shape, dt, offset=at)

        TB = 4 * S
        w_raw = [sb(f"w_raw{i}", [P, KD * CW], F32) for i in range(2)]
        w_hi = [sb(f"w_hi{i}", [P, KD * CW], F32R) for i in range(2)]
        w_lo = [sb(f"w_lo{i}", [P, KD * CW], F32R) for i in range(2)]
        hT = sb("hT", [P, KD, S], F32)
        u_hi = sb("u_hi", [P, KD, S], F32R)
        u_lo = sb("u_lo", [P, KD, S], F32R)
        region = place[0]
        s_hi = sb("s_hi", [P, KF, S], F32R)
        s_lo = sb("s_lo", [P, KF, S], F32R)
        place[0] += 10 * TB
        tables_at = place[0]
        tables = sb("tables", [P, 5 * P], F32)
        ident, head_ones, hidden = (tables[:, i * P:(i + 1) * P] for i in range(3))
        chunk_causal, ones = tables[:, 3 * P:4 * P], tables[:, 4 * P:5 * P]
        vec = sb("vec", [P, 58], F32)
        gains, bg = vec[:, 0:24].rearrange("p (n k) -> p n k", n=3), vec[:, 24:48]
        ba, gg, head_gains = vec[:, 48:52], vec[:, 52:54], vec[:, 54:58]
        iw = sb("iw", [P, NT, 8], F32)
        st = sb("st", [P, 64], F32)
        token_root = st[:, 44:48]
        top8 = sb("top8", [P, 3, 8], F32)
        wa2_sb = sb("wa2_sb", [P, P], F32)
        decay = sb("decay", [P, NCH], F32)
        assert place[0] <= nc.sbuf_usable_end, (place[0], nc.sbuf_usable_end)

        def tile(name, i, n=1, shape=None):
            return nc.alloc_sbuf_tensor_at(name, shape or [P, int(n * S)], F32, offset=region + i * TB)

        x_in_sb = [tile(f"x_in_sb{t_}", 24 + 2 * t_, 2) for t_ in range(NT)]
        onehot_sb, mask_sb, rv_sb = tile("onehot_sb", 8, 2), tile("mask_sb", 10, 2), tile("rv_sb", 50, 2)
        relb_sb, vec_rows = tile("relb_sb", 12), tile("vec_rows", 13)
        xn = [tile(f"xn{t_}", 32 + 2 * t_, 2) for t_ in range(NT)]
        xg = [tile(f"xg{i}", 40 + i, 1, [P, KD // 2, P]) for i in range(4)]
        sq = [tile("sq0", 44), tile("sq1", 45)]
        sq_sum, rstd = tile("sq_sum", 46), tile("rstd", 47)
        normed = [tile("normed0", 48), tile("normed1", 49)]
        qa = [tile(f"qa{i}", 2 + i) for i in range(6)]
        ka = [tile(f"ka{i}", 24 + i) for i in range(6)]
        va = tile("va", 44, 6, [P, NT, 768])
        cq = [tile(f"cq{i}", 16 + i) for i in range(6)]
        iq = [tile(f"iq{i}", 38 + i) for i in range(4)]
        ck, ik = tile("ck", 42), tile("ik", 43)
        cv = nc.alloc_sbuf_tensor_at("cv", [P, NT, HD], F32, offset=region + 37 * TB + TB // 2)
        al = tile("al", 31)
        head_tmp = tile("head_tmp", 53)
        bqk = [tile(f"bqk{i}", 44 + i) for i in range(8)]
        bv = [tile(f"bv{i}", (24, 26, 28, 6)[i], 2) for i in range(NT)]
        sa = [tile("sa0", 50, 3), tile("sa1", 8, 3)]
        pta = [tile("pta0", 32, 3), tile("pta1", 35, 2.5)]
        bias_a = [[tile(f"bias_a{r}{g}", (11, 12, 13, 14, 15, 30)[3 * r + g]) for g in range(3)] for r in range(2)]
        sc = [tile(f"sc{i}", (52, 53, 8, 41)[i]) for i in range(4)]
        ptc = [tile(f"ptc{i}", 38 + i) for i in range(3)]
        bias_c = [tile(f"bias_c{i}", (5, 9, 30, 43)[i]) for i in range(4)]
        score = [None, tile("score1", 2), tile("score2", 3), tile("score3", 4)]
        chosen = [None] + [nc.alloc_sbuf_tensor_at(f"chosen{i - 1}", [P, S], F32R, offset=region + i * TB)
                           for i in (2, 3, 4)]
        ident_r = nc.alloc_sbuf_tensor_at("ident_r", [P, P], F32R, offset=tables_at + 4 * 2 * P)
        relu = [tile("relu0", 52), tile("relu1", 53)]
        g_t = [tile(f"g_t{i}", (2, 3, 4, 5, 20, 21)[i]) for i in range(6)]
        g_state = [tile(f"g_state{i}", 16 + i, 1, [P, 2, GV]) for i in range(4)]
        g_reset = tile("g_reset", 9)
        part = [tile(f"part{d}", 38 + d if d < 6 else 46 + d) for d in range(KD)]
        gate_t = [tile("gate_t0", 8), tile("gate_t1", 30)]
        silu_r = [tile(f"silu_r{i}", 16 + i) for i in range(4)]
        gate_b_t = [tile(f"gate_b_t{i}", 44 + i) for i in range(4)]
        silu_g = [tile("silu_g0", 44), tile("silu_g1", 45)]
        prod = [tile("prod0", 46, 1, [P, 1, S]), tile("prod1", 48, 1, [P, 1, S])]
        sq_row = [tile(f"sq_row{c}", 44 + c, 1, [P, 1, S]) for c in range(2)]
        normed_row = [tile(f"normed_row{c}", 48 + c, 1, [P, 1, S]) for c in range(2)]
        p_sb = tile("p_sb", 50, 2, [P, NT, PLE])
        p_hi, p_lo = (nc.alloc_sbuf_tensor_at(n_, [P, 2, S], F32R, offset=region + i * TB)
                      for n_, i in (("p_hi_sb", 50), ("p_lo_sb", 52)))
        pp = [tile(f"pp{t_}", 2 + 2 * t_, 2) for t_ in range(NT)]
        sig = [tile("sig0", 12, 1, [P, 2, CW]), tile("sig1", 13, 1, [P, 2, CW])]
        out_sb = [tile(f"out_sb{i}", 14 + i, 1, [P, 2, CW]) for i in range(8)]

        merged = [(s_hi[:, i, :], s_lo[:, i, :]) for i in (10, 11, 12, 13, 14, 15, 0, 1)]

        bank = [ctx.enter_context(nc.psum_tensor(f"bank{i}", [P, S], F32)) for i in range(8)]
        QK, TR, OUT, MISC = (2, 3), (4, 5), 6, 7

        def out_bank(u):
            return bank[MISC if u >= 16 and u // 8 % 2 else OUT]


        names = """const_in mix_in vec_in token_ss xn_done xt_done sq_done sum_done ss_done rstd_done normed_done u_hi_done
            u_lo_done hi_ready lo_ready w_used proj_done head_sq head_ss head_rstd head_normed rv_mm
            rv_done qk_done s_ready exp_done p_ready t_done t_free pv_done o_hi_done o_lo_done relu_used
            sel_done gl_L gl_abs gl_min gl_ln gl_scan gl_e gl_qk gl_tk gl_kend gl_att gl_attT gl_u
            gl_state gl_o gl_osq gl_ss gl_r gl_out part_done r_prod r_hi r_lo m_sum m_hi m_lo h2_done
            ff_silu ff_scaled ff_hi ff_lo p_in pt_done p_hi p_lo ht_done out_ready out_done dve_step
            act_step small_done topk_done reset_done scratch_done wa2_in vec_turned""".split()
        sem = {n: ctx.enter_context(nc.semaphore(n)) for n in names}
        raw_in = [ctx.enter_context(nc.semaphore(f"raw_in{i}")) for i in range(2)]
        proj_free = [ctx.enter_context(nc.semaphore(f"proj_free{i}")) for i in range(4)]
        qk_free = [ctx.enter_context(nc.semaphore(f"qk_free{i}")) for i in range(2)]
        x_in = [ctx.enter_context(nc.semaphore(f"x_in{i}")) for i in range(NT)]
        bias_a_in = [ctx.enter_context(nc.semaphore(f"bias_a_in{i}")) for i in range(2)]
        bias_c_in = [ctx.enter_context(nc.semaphore(f"bias_c_in{i}")) for i in range(4)]

        def rows(name):
            return t[name][0].rearrange("(k p) n -> p k n", p=P)

        w_in = rows("w_in")

        def cols(w, c0, n=CW):
            return w[:, :, c0:c0 + n]

        slots, groups, g_of = [], [], {}

        def slot(kc, width, loads):
            slots.append((kc, width, loads))
            return len(slots) - 1

        def group(key, n, kind, x=None, c0=0, m=P, kc=KD, toks=None, nc_=None):
            g_of[key] = len(groups)
            groups.append(dict(slot=n, kind=kind, x=x, c0=c0, m=m, kc=kc, toks=toks, n=nc_))

        def u_tile(k):
            return u_hi[:, k, :], u_lo[:, k, :]

        def o_tile(i):
            return s_hi[:, i, :], s_lo[:, i, :]

        def feature_slots(key, w, c0, count, kc=KD, x=u_tile, first=0):
            for i in range(first, count):
                n = slot(kc, CW, [(0, cols(w, c0 + CW * i))])
                for c in range(2):
                    group((key, 2 * i + c), n, "feat", x, P * c, P, kc)

        def token_slots(key, w, c0, count, first=0):
            for i in range(first, count):
                n = slot(KD, CW, [(0, cols(w, c0 + CW * i))])
                for c in range(2):
                    group((key, 2 * i + c), n, "tok", u_tile, 0, toks=(2 * c, 2 * c + 1), nc_=CW)

        token_slots("av", w_in, O_AV, 1)
        feature_slots("aq", w_in, O_AQ, 3)
        feature_slots("ak", w_in, O_AK, 3)
        token_slots("av", w_in, O_AV, 3, first=1)
        T1_GROUPS = len(groups)
        n_ = slot(KD, AVI, [(0, cols(w_in, O_AL, 16)), (16, cols(w_in, O_CV, HD)), (16 + HD, cols(w_in, O_IW, 8))])
        group(("al", 0), n_, "feat", u_tile, 0, AVI)
        feature_slots("iq", w_in, O_IQ, 1)
        group(("cviw", 0), len(slots) - 1, "turn")
        feature_slots("iq", w_in, O_IQ, 2, first=1)
        n_ = slot(KD, CW, [(HD * i, cols(w_in, (O_CK, O_CK, O_IK, O_IK)[i], HD)) for i in range(4)])
        group(("ck", 0), n_, "feat", u_tile, 0)
        group(("ik", 0), n_, "feat", u_tile, P)
        feature_slots("cq", w_in, O_CQ, 3)
        T2_GROUPS = len(groups)
        feature_slots("bq", w_in, O_BQ, 2)
        feature_slots("bk", w_in, O_BK, 2)
        token_slots("bv", w_in, O_BV, 4)
        T3_GROUPS = len(groups)
        B_IN_C = T3_GROUPS - 2
        w_gate = rows("w_gate")
        feature_slots("ga", w_gate, 0, 4)
        w_oc, w_ob, w_oo = rows("w_out_c"), rows("w_out_b"), rows("w_o")
        for j_ in range(4):
            for key, w, kc, x in (("gc", w_gate, KD, u_tile), ("yc", w_oc, 6, lambda k: o_tile(10 + k))):
                n_ = slot(kc, CW, [(0, cols(w, (2 * D if key == "gc" else 0) + CW * j_))])
                for c in range(2):
                    group((key, 2 * j_ + c), n_, "feat", x, P * c, P, kc)
                if j_ == 0 and key == "gc":
                    n_ = slot(2, D, [(0, rows("w_out_a"))])
                    for d_ in range(KD):
                        group(("ya", d_), n_, "feat", lambda k: o_tile(k), P * d_, P, 2)
        T4_GROUPS = len(groups)
        feature_slots("br", w_in, O_BR, 4)
        for j_ in range(4):
            for key, w, x in (("gb", w_gate, u_tile), ("yb", w_ob, lambda k: o_tile(2 + k))):
                n_ = slot(KD, CW, [(0, cols(w, (D if key == "gb" else 0) + CW * j_))])
                for c in range(2):
                    group((key, 2 * j_ + c), n_, "feat", x, P * c, P, KD)
        feature_slots("wo", w_oo, 0, 4, x=lambda k: merged[k])
        PRE_SLOTS, PRE_GROUPS = len(slots), len(groups)
        assert PRE_SLOTS % 2 == 1

        kind_of = {g: key for key, g in g_of.items()}
        last_group = {}
        uses, bank_of, use_of = [0] * 4, [], []
        for g, gr in enumerate(groups):
            b_ = g % 2 if g < T4_GROUPS else g % 4
            bank_of.append(b_)
            use_of.append(uses[b_])
            if kind_of[g][0] != "wo":
                uses[b_] += 1
            last_group[gr["slot"]] = g
        first_group = {}
        for g, gr in enumerate(groups):
            first_group.setdefault(gr["slot"], g)
        landed, total_ = [], [0, 0]
        for n, (_, _, loads) in enumerate(slots):
            total_[n % 2] += len(loads)
            landed.append(total_[n % 2])

        FFN_N, DOWN_N = PRE_SLOTS, PRE_SLOTS + 2 * (FF // CW)
        DOWN_ROWS = ((0, 6), (6, 6), (12, 5), (17, 5))
        PLE_N = DOWN_N + 4 * (D // CW)
        FFN_G, DOWN_G = PRE_GROUPS, PRE_GROUPS + 4 * (FF // CW)
        PLE_G = DOWN_G + 2 * (D // CW)
        FI, DI = FF // CW, D // CW

        def landed_value(n, i=0):
            if n < PRE_SLOTS:
                return 16 * landed[n]
            return 16 * (total_[n % 2] + (n - PRE_SLOTS) // 2 + 1) + 16 * i

        def raw_view(n, kc, width):
            return w_raw[n % 2][:, 0:kc * width].rearrange("p (k c) -> p k c", k=kc)

        def part_views(n, kc, width):
            return (w_hi[n % 2][:, 0:kc * width].rearrange("p (k c) -> p k c", k=kc),
                    w_lo[n % 2][:, 0:kc * width].rearrange("p (k c) -> p k c", k=kc))

        def wait_slot_used(eng, n):
            if n >= 0:
                eng.wait_ge(sem["proj_done"], last_group[n] + 1)

        units, n_qk, n_tr, n_ready = [], 0, 0, 0
        for u in range(64):
            if u < 16:
                s_, b = u // 4, u % 4
                half = s_ % 2
                kb0 = [max(b - 1, 0), 0, 0]
                subs, blocks, at = [], [], 0
                for g in range(A_GROUPS):
                    hd_ = 4 * g + s_
                    k0, k1 = kb0[g], b + 1
                    subs.append(dict(q=qa[hd_ // 2], k=ka[hd_ // 2], k0=k0 * P, k1=k1 * P, at=at,
                                     bias=bias_a[s_ % 2][g]))
                    for kb in range(k0, k1):
                        blocks.append((at + (kb - k0) * P, va[:, kb, HD * hd_:HD * hd_ + HD]))
                    at += (k1 - k0) * P
                S_, PT_ = sa[u % 2], pta[u % 2]
            else:
                h, b = (u - 16) // 4, (u - 16) % 4
                half = h % 2
                subs = [dict(q=cq[h // 2], k=ck, k0=0, k1=(b + 1) * P, at=0, bias=bias_c[h % 4])]
                blocks = [(kb * P, cv[:, kb, :]) for kb in range(b + 1)]
                at = (b + 1) * P
                S_, PT_ = sc[u % 4], ptc[u % 3]
            if u == 16:
                n_qk += 3 * IDX_HEADS
            chunks = [blocks[i:i + 4] for i in range(0, len(blocks), 4)]
            units.append(dict(b=b, half=half, subs=subs, chunks=chunks, width=at, S=S_, PT=PT_, qk0=n_qk,
                              tr0=n_tr))
            if u >= 16:
                units[-1]["ready"] = (qk_free[n_qk % 2], n_qk // 2 + 1)
            else:
                n_ready += 1
                units[-1]["ready"] = (sem["s_ready"], n_ready)
            n_qk += len(subs)
            n_tr += len(chunks)
        IDX_QK0 = 48
        idx = [(b, h) for b in (1, 2, 3) for h in range(IDX_HEADS)]
        EARLY = (12, 20)
        pair_tile = [0, 1, 10, 11, 12, 13, 14, 15]

        def ple_free(g):
            return uses[g % 4] + FI + g // 4

        chains = ([(g_of["aq", i], qa[i], 0) for i in range(6)] + [(g_of["ak", i], ka[i], 1) for i in range(6)]
                  + [(g_of["ck", 0], ck, 3)] + [(g_of["cq", i], cq[i], 2) for i in range(6)])
        chain_at = {c[0]: i for i, c in enumerate(chains)}

        STEPS = 5 * GH
        t4 = list(range(T3_GROUPS + 2, T4_GROUPS))
        work = [groups[g]["kc"] for g in t4]
        share = np.cumsum(T4_SHARE * GH) / (GH * sum(T4_SHARE)) * sum(work)
        t4_step, at, done_ = [], 0, 0
        for j in range(STEPS):
            t4_step.append([])
            while at < len(t4) and done_ + work[at] / 2 <= share[j]:
                t4_step[j].append(t4[at])
                done_ += work[at]
                at += 1
        assert at == len(t4)

        VECS = 16 * 9
        MIX = 16 * 2
        st_ = lambda u, i: st[:, (u % 4) * 8 + i:(u % 4) * 8 + i + 1]

        block = ctx.enter_context(nc.Block())

        @block.sync
        def _(sp):
            def load(n):
                kc, width, loads = slots[n]
                if n >= 2:
                    sp.wait_ge(sem["hi_ready"], n - 1)
                    sp.wait_ge(sem["lo_ready"], n - 1)
                for c0, src in loads:
                    sp.dma_start(raw_view(n, kc, width)[:, :, c0:c0 + src.shape[2]], src).then_inc(raw_in[n % 2], 16)

            x_v = t["x"][0].rearrange("(t p) d -> t p d", p=P)
            for tb in range(NT):
                sp.dma_start(x_in_sb[tb][:, :], x_v[tb]).then_inc(x_in[tb], 16)
                if tb == 1:
                    load(0)
            def by_row(r, name):
                src = t[name][0].rearrange("(k p) -> k p", p=P)
                sp.dma_start(vec_rows[r:r + src.shape[0], 0:P], src).then_inc(sem["vec_in"], 16)

            by_row(8, "norm_ffn")
            by_row(16, "norm_ple")
            by_row(24, "b_gate")
            by_row(48, "b_alpha")
            by_row(52, "gla_norm")
            for i, name in enumerate(("qn_a", "kn_a", "qn_c", "kn_c")):
                src = t[name]
                sp.dma_start(vec_rows[54 + i:55 + i, 0:P].rearrange("r (h c) -> r h c", h=2),
                             bass.AP(tensor=src.tensor, offset=src.offset, ap=[[HD, 1], [0, 2], [1, HD]])).then_inc(
                                 sem["vec_in"], 16)
            for dst, src in ((relb_sb[0:BUCKETS, 0:24], "rel_bias"), (onehot_sb[0:BUCKETS, 0:RV], "c_onehot"),
                             (mask_sb[0:24, 0:RV], "c_mask")):
                sp.dma_start(dst, t[src]).then_inc(sem["const_in"], 16)
            for n in range(1, PRE_SLOTS):
                load(n)

            w_fg, w_fu, w_fd = rows("w_ffn_gate"), rows("w_ffn_up"), rows("w_ffn_down")
            with sp.Fori(0, FI) as i:
                for c, w in enumerate((w_fg, w_fu)):
                    sp.wait_ge(sem["hi_ready"], i * 2 + (FFN_N + c - 1))
                    sp.wait_ge(sem["lo_ready"], i * 2 + (FFN_N + c - 1))
                    sp.dma_start(raw_view(FFN_N + c, KD, CW), w[:, :, bass.ds(i * CW, CW)]).then_inc(
                        raw_in[(FFN_N + c) % 2], 16)
            with sp.Fori(0, DI) as i:
                for c, (k0, kc) in enumerate(DOWN_ROWS):
                    sp.wait_ge(sem["hi_ready"], i * 4 + (DOWN_N + c - 1))
                    sp.wait_ge(sem["lo_ready"], i * 4 + (DOWN_N + c - 1))
                    sp.dma_start(raw_view(DOWN_N + c, kc, CW), w_fd[:, k0:k0 + kc, bass.ds(i * CW, CW)]).then_inc(
                        raw_in[(DOWN_N + c) % 2], 16)
            w_pp, w_pg = rows("w_ple_proj"), rows("w_ple_gate")
            for j in range(5):
                n = PLE_N + j
                sp.wait_ge(sem["hi_ready"], n - 1)
                sp.wait_ge(sem["lo_ready"], n - 1)
                if j == 0:
                    sp.dma_start(raw_view(n, 2, D), w_pp).then_inc(raw_in[n % 2], 16)
                else:
                    sp.dma_start(raw_view(n, KD, CW), cols(w_pg, CW * (j - 1))).then_inc(raw_in[n % 2], 16)
            out_v = out[0].rearrange("(t p) d -> p t d", p=P)
            for i in range(8):
                j, tp = i // 2, i % 2
                sp.wait_ge(sem["out_ready"], i + 1)
                sp.dma_start(out_v[:, 2 * tp:2 * tp + 2, CW * j:CW * j + CW], out_sb[i][:, :, :]).then_inc(
                    sem["out_done"], 16)
            sp.wait_ge(sem["out_done"], 8 * 16)

        @block.gpsimd
        def _(pool):
            def lo(n, kc, width, i2=0):
                pool.wait_ge(sem["hi_ready"], i2 + (n + 1))
                r = slice(0, kc * width)
                pool.tensor_tensor(w_lo[n % 2][:, r], w_raw[n % 2][:, r], w_hi[n % 2][:, r].bitcast(F32),
                                   ALU.subtract).then_inc(sem["lo_ready"], 1)

            for n in range(PRE_SLOTS):
                wait_slot_used(pool, n - 2)
                lo(n, slots[n][0], slots[n][1])
            with pool.Fori(0, FI) as i:
                for c in range(2):
                    lo(FFN_N + c, KD, CW, i * 2)
            with pool.Fori(0, DI) as i:
                for c, (_, kc) in enumerate(DOWN_ROWS):
                    lo(DOWN_N + c, kc, CW, i * 4)
            for j in range(5):
                lo(PLE_N + j, *((2, D) if j == 0 else (KD, CW)))

        @block.scalar
        def _(act):
            own = [0]

            def link(ins):
                own[0] += 1
                ins.then_inc(sem["act_step"], 1)
                act.wait_ge(sem["act_step"], own[0])

            def hi(n, kc=None, width=None, i_landed=0):
                if kc is None:
                    kc, width = slots[n][:2]
                act.wait_ge(raw_in[n % 2], landed_value(n) + i_landed)
                r = slice(0, kc * width)
                act.copy(w_hi[n % 2][:, r], w_raw[n % 2][:, r]).then_inc(sem["hi_ready"], 1)

            begun = set()

            def next_hi(g):
                n = groups[g]["slot"]
                if first_group[n] == g and g not in begun:
                    begun.add(g)
                    if n + 1 < PRE_SLOTS:
                        wait_slot_used(act, n - 1)
                        hi(n + 1)
                    else:
                        wait_slot_used(act, n - 1)
                        hi(FFN_N, KD, CW)

            def dma(dst, src, s):
                act.dma_start(dst, src).then_inc(s, 16)

            nc.scalar.preload_act_table_set(LN_EXP)
            dma(tables[:, :], t["c_tables"], sem["mix_in"])
            dma(vec_rows[0:8, 0:P], t["norm_mix"][0].rearrange("(k p) -> k p", p=P), sem["mix_in"])
            dma(wa2_sb[0:16, :], t["w_alpha2"][0, :, 0:P], sem["wa2_in"])

            def root(j, dst, total):
                act.wait_ge(sem["ss_done"], j)
                link(act.activation(dst, total, ACT.Ln, scale=1.0 / D, bias=st[:, 40:41]))
                act.activation(dst, dst, ACT.Exp, scale=-0.5).then_inc(sem["rstd_done"], 1)

            def token_norm(tb):
                ss = st[:, tb:tb + 1]
                act.wait_ge(x_in[tb], 16)
                link(act.activation(xn[tb][:, :], x_in_sb[tb][:, :], ACT.Square, accum_out=ss))
                link(act.activation(ss, ss, ACT.Ln, scale=1.0 / D, bias=st[:, 40:41]))
                act.activation(ss, ss, ACT.Exp, scale=-0.5).then_inc(sem["token_ss"], 1)

            def u_hi_part(q):
                tb, half = q // 2, q % 2
                act.wait_ge(sem["normed_done"], q + 1)
                act.copy(u_hi[:, 4 * half:4 * half + 4, P * tb:P * tb + P], xg[q % 4][:, :, :]).then_inc(
                    sem["u_hi_done"], 1)

            act.wait_ge(sem["small_done"], 1)
            for tb in (0, 1):
                token_norm(tb)
            hi(0)
            for q in range(4):
                u_hi_part(q)
            for tb in (2, 3):
                token_norm(tb)
            for q in range(4, 8):
                u_hi_part(q)

            def load_bias(dst, head, s):
                src = t["c_scratch"]
                act.dma_start(dst[:, :], bass.AP(tensor=src.tensor, offset=head * RV, ap=[[1, P], [1, S]])).then_inc(
                    s, 16)

            def load_bias_a(s_):
                for g in range(A_GROUPS):
                    load_bias(bias_a[s_ % 2][g], 4 * g + s_, bias_a_in[s_ % 2])

            def head_norm(g):
                if g - 1 in chain_at:
                    c = chain_at[g - 1]
                    act.wait_ge(sem["head_ss"], c + 1)
                    link(act.activation(head_tmp[:, :], bank[MISC][:, :], ACT.Ln, scale=1.0 / HD, bias=st[:, 40:41]))
                    act.activation(head_tmp[:, :], head_tmp[:, :], ACT.Exp, scale=-0.5).then_inc(sem["head_rstd"], 1)
                if g in chain_at:
                    c = chain_at[g]
                    act.wait_ge(proj_free[bank_of[g]], use_of[g] + 1)
                    if c:
                        act.wait_ge(sem["head_normed"], c)
                    act.activation(head_tmp[:, :], chains[c][1][:, :], ACT.Square).then_inc(sem["head_sq"], 1)

            def take_bank(g, dst, src=None):
                act.wait_ge(sem["proj_done"], g + 1)
                act.copy(dst, bank[bank_of[g]][:, :] if src is None else src).then_inc(proj_free[bank_of[g]], 1)

            def tok_view(g, w=CW):
                return bank[bank_of[g]][:, 0:2 * w].rearrange("p (t c) -> p t c", t=2)

            for g in range(T1_GROUPS):
                next_hi(g)
                if g == 2:
                    act.wait_ge(sem["rv_done"], 2)
                    act.dma_start(t["c_scratch"], rv_sb[0:24, 0:RV]).then_inc(sem["scratch_done"], 16)
                if g == 9:
                    act.wait_ge(sem["scratch_done"], 16)
                    act.wait_ge(sem["xt_done"], 2 * KD)
                    load_bias_a(0)
                    load_bias_a(1)
                head_norm(g)
                if kind_of[g][0] == "av":
                    i, c = kind_of[g][1] // 2, kind_of[g][1] % 2
                    take_bank(g, va[:, 2 * c:2 * c + 2, CW * i:CW * i + CW], tok_view(g))

            def exp(u):
                U = units[u]
                act.wait_ge(*U["ready"])
                act.activation(U["S"][:, 0:U["width"]], U["S"][:, 0:U["width"]], ACT.Exp, bias=st_(u, 3), scale=-1.0,
                               accum_out=st_(u, 4)).then_inc(sem["exp_done"], 1)

            def take_probs(u):
                U = units[u]
                if u >= 2:
                    act.wait_ge(sem["pv_done"], u - 1 if u < 18 else u - 2)
                for c, ch in enumerate(U["chunks"]):
                    k = U["tr0"] + c
                    act.wait_ge(sem["t_done"], k + 1)
                    w = P * len(ch)
                    act.copy(U["PT"][:, 4 * P * c:4 * P * c + w], bank[TR[k % 2]][:, 0:w]).then_inc(sem["t_free"], 1)

            def out_hi(u):
                if u % 8 == 7:
                    act.wait_ge(sem["pv_done"], u + 1)
                    act.copy(s_hi[:, pair_tile[u // 8], :], out_bank(u)[:, :]).then_inc(sem["o_hi_done"], 1)

            for i in range(18):
                g = T1_GROUPS + i
                if i >= 3:
                    out_hi(i - 3)
                if i < 16:
                    next_hi(g)
                    exp(i)
                    if i % 4 == 3 and i // 4 + 2 < A_SLOTS:
                        load_bias_a(i // 4 + 2)
                if g <= T2_GROUPS:
                    head_norm(g)
                if 1 <= i <= 16:
                    take_probs(i - 1)
            out_hi(15)

            def take_b(g):
                next_hi(g)
                key, i = kind_of[g]
                if key in ("bq", "bk"):
                    take_bank(g, bqk[2 * i + (key == "bk")][:, :])
                else:
                    j, c = i // 2, i % 2
                    act.wait_ge(sem["proj_done"], g + 1)
                    act.copy(bv[2 * c][:, CW * j:CW * j + CW], bank[bank_of[g]][:, 0:CW])
                    act.copy(bv[2 * c + 1][:, CW * j:CW * j + CW], bank[bank_of[g]][:, CW:2 * CW]).then_inc(
                        proj_free[bank_of[g]], 1)

            act.wait_ge(sem["pv_done"], 16)
            for e, (b, h) in enumerate(idx):
                k = IDX_QK0 + e
                act.wait_ge(sem["qk_done"], k + 1)
                if e >= 2:
                    act.wait_ge(sem["relu_used"], e - 1)
                w = P * (b + 1)
                act.activation(relu[e % 2][:, 0:w], bank[QK[k % 2]][:, 0:w], ACT.Relu).then_inc(qk_free[k % 2], 1)
                if e % 6 == 5:
                    take_b(T2_GROUPS + e // 6)
                    next_hi(T2_GROUPS + e // 6 + 2)
            for h in range(4):
                load_bias(bias_c[h], C_HEADS + h, bias_c_in[h])
            for g in range(T2_GROUPS + 4, B_IN_C):
                take_b(g)
                if g + 2 < B_IN_C:
                    next_hi(g + 2)
            for j in range(53):
                if j < 48:
                    exp(16 + j)
                    if j % 4 == 3 and j // 4 + 4 < C_HEADS:
                        h = j // 4 + 4
                        load_bias(bias_c[h % 4], C_HEADS + h, bias_c_in[h % 4])
                if j % 2 == 0 and B_IN_C + j // 2 < T3_GROUPS:
                    take_b(B_IN_C + j // 2)
                if j in (EARLY[0], EARLY[1] + 2):
                    next_hi(T3_GROUPS if j == EARLY[0] else T3_GROUPS + 2)
                if 3 <= j <= 50:
                    take_probs(16 + j - 3)
                if j >= 5:
                    out_hi(16 + j - 5)

            def gla(h, stage):
                if stage in (0, 4):
                    nc.scalar.preload_act_table_set(LN_EXP)
                if stage == 0:
                    act.wait_ge(sem["gl_L"], h + 1)
                    if h:
                        act.wait_ge(sem["gl_ss"], h)
                    act.activation(g_t[0][:, :], bank[2][:, :], ACT.Abs, bias=ba[:, h:h + 1]).then_inc(sem["gl_abs"], 1)
                    act.wait_ge(sem["gl_abs"], h + 1)
                    link(act.activation(g_t[0][:, :], g_t[0][:, :], ACT.Exp, scale=-1.0))
                    act.activation(g_t[0][:, :], g_t[0][:, :], ACT.Ln, bias=st[:, 41:42]).then_inc(sem["gl_ln"], 1)
                    act.wait_ge(sem["gl_scan"], h + 1)
                    cum = g_t[2]
                    act.activation(g_t[3][:, :], cum[:, :], ACT.Exp, scale=1.0 / TAU).then_inc(sem["gl_e"], 1)
                    act.activation(g_t[4][:, :], cum[:, :], ACT.Exp, scale=-1.0 / TAU).then_inc(sem["gl_e"], 1)
                    act.activation(g_t[1][:, :], g_t[0][:, :], ACT.Exp, scale=1.0 / TAU).then_inc(sem["gl_e"], 1)
                    if h:
                        act.wait_ge(sem["gl_state"], (NCH - 1) * h)
                    act.activation(decay[:, :], cum[:, CH - 1:S:CH], ACT.Exp, scale=1.0 / TAU).then_inc(sem["gl_e"], 1)
                    if h + 1 < GH:
                        dma(wa2_sb[0:16, :], t["w_alpha2"][0, :, P * (h + 1):P * (h + 2)], sem["wa2_in"])
                elif stage == 1:
                    act.wait_ge(sem["gl_tk"], h + 1)
                    act.copy(g_t[1][:, :], bank[2][:, :]).then_inc(sem["gl_kend"], 1)
                elif stage == 3:
                    for e in range(2):
                        act.wait_ge(sem["gl_o"], 2 * h + e + 1)
                        act.copy(g_t[4 + e][:, :], bank[(OUT, MISC)[e]][:, :]).then_inc(sem["gl_osq"], 1)
                        act.wait_ge(sem["gl_osq"], 4 * h + 2 * e + 1)
                        act.activation(g_t[e][:, :], g_t[4 + e][:, :], ACT.Square).then_inc(sem["gl_osq"], 1)
                elif stage == 4:
                    act.wait_ge(sem["gl_ss"], h + 1)
                    link(act.activation(g_t[2][:, :], bank[2][:, :], ACT.Ln, scale=1.0 / GV, bias=st[:, 40:41]))
                    act.activation(g_t[2][:, :], g_t[2][:, :], ACT.Exp, scale=-0.5).then_inc(sem["gl_r"], 1)

            def gate_exp(g):
                key, d = kind_of[g]
                if key not in ("ga", "gc", "br", "gb"):
                    return
                dst, bias = {"ga": lambda: (part[d], bg[:, d:d + 1]),
                             "gc": lambda: (gate_t[d % 2], bg[:, 16 + d:17 + d]),
                             "br": lambda: (silu_r[d % 4], 0.0),
                             "gb": lambda: (gate_b_t[d % 4], bg[:, 8 + d:9 + d])}[key]()
                if key == "gc" and d >= 2:
                    act.wait_ge(sem["part_done"], d - 1)
                if key == "br" and d >= 4:
                    act.wait_ge(sem["r_lo"], d - 3)
                if key == "gb" and d == 0:
                    act.wait_ge(sem["r_lo"], KD)
                if key == "gb" and d >= 4:
                    act.wait_ge(sem["m_lo"], d - 3)
                act.wait_ge(sem["proj_done"], g + 1)
                act.activation(dst[:, :], bank[bank_of[g]][:, :], ACT.Silu if key == "br" else ACT.Sigmoid,
                               bias=bias).then_inc(proj_free[bank_of[g]], 1)

            nc.scalar.preload_act_table_set("sigmoid_and_others")
            act.wait_ge(sem["pv_done"], 64)
            gate_exp(T3_GROUPS)
            gate_exp(T3_GROUPS + 1)
            act.wait_ge(sem["o_lo_done"], 8)
            for j in range(STEPS):
                if j and t4_step[j]:
                    next_hi(t4_step[j][0])
                gla(j // 5, j % 5)
                for i, g in enumerate(t4_step[j]):
                    if i:
                        next_hi(g)
                    gate_exp(g)

            for g in range(T4_GROUPS, g_of["wo", 0]):
                next_hi(g)
                if kind_of[g][0] == "gb" and kind_of[g][1] == 0:
                    act.wait_ge(sem["r_prod"], KD)
                    act.copy(s_hi[:, 2 + KD - 1, :], silu_r[(KD - 1) % 4][:, :]).then_inc(sem["r_hi"], 1)
                gate_exp(g)
                key, d = kind_of[g]
                if key == "br" and d >= 1:
                    act.wait_ge(sem["r_prod"], d)
                    act.copy(s_hi[:, 2 + d - 1, :], silu_r[(d - 1) % 4][:, :]).then_inc(sem["r_hi"], 1)
                if key == "yb":
                    act.wait_ge(sem["m_sum"], d + 1)
                    act.copy(merged[d][0], gate_b_t[d % 4][:, :]).then_inc(sem["m_hi"], 1)
            dma(p_sb[:, :, :], t["p"][0, 0].rearrange("(t p) c -> p t c", p=P), sem["p_in"])

            for d in range(KD):
                next_hi(g_of["wo", d])
                act.wait_ge(sem["normed_done"], KD + d + 1)
                act.copy(u_hi[:, d, :], normed[d % 2][:, :]).then_inc(sem["u_hi_done"], 1)
                if d == KD - 1:
                    act.wait_ge(sem["proj_done"], FFN_G)
                    hi(FFN_N + 1, KD, CW)
                if d >= 2:
                    act.wait_ge(sem["sum_done"], d - 1)
                act.activation(sq[d % 2][:, :], hT[:, d, :], ACT.Square).then_inc(sem["sq_done"], 1)
            root(1, rstd[:, :], bank[MISC][:, :])

            def ffn(i, first=False, last=False):
                if not first:
                    act.wait_ge(sem["proj_done"], i * 4 + FFN_G)
                    hi(FFN_N + 1, KD, CW, i * 16)
                for c in range(2):
                    act.wait_ge(proj_free[c], i + (uses[c] + 1))
                    act.activation(silu_g[c][:, :], silu_g[c][:, :], ACT.Silu).then_inc(sem["ff_silu"], 1)
                act.wait_ge(sem["proj_done"], i * 4 + (FFN_G + 2))
                if last:
                    hi(DOWN_N, DOWN_ROWS[0][1], CW)
                else:
                    hi(FFN_N, KD, CW, (i + 1) * 16)
                for c in range(2):
                    act.wait_ge(proj_free[2 + c], i + (uses[2 + c] + 1))
                    act.copy(s_hi[:, bass.ds(i * 2 + c, 1), :], prod[c][:, :, :]).then_inc(sem["ff_hi"], 1)

            ffn(0, first=True)
            with act.Fori(1, FI - 1) as i:
                ffn(i)
            ffn(FI - 1, last=True)

            for k in range(2):
                act.wait_ge(sem["pt_done"], 2)
                act.copy(p_hi[:, k, :], bank[TR[k]][:, :]).then_inc(sem["p_hi"], 1)

            def rows_hi(i):
                for c in range(2):
                    act.wait_ge(sem["normed_done"], i * 2 + (2 * KD + c + 1))
                    act.copy(u_hi[:, bass.ds(i * 2 + c, 1), :], normed_row[c][:, :, :]).then_inc(
                        sem["u_hi_done"], 1)
                    act.wait_ge(sem["sum_done"], i * 2 + (KD + c - 1))
                    act.activation(sq_row[c][:, :, :], hT[:, bass.ds(i * 2 + c, 1), :], ACT.Square).then_inc(
                        sem["sq_done"], 1)

            def down(i, first=False, last=False):
                for c in range(4):
                    if c == 0:
                        act.wait_ge(sem["proj_done"], i * 2 + DOWN_G)
                    else:
                        act.wait_ge(sem["w_used"], i * 3 + c)
                    if c < 3:
                        hi(DOWN_N + c + 1, DOWN_ROWS[c + 1][1], CW, i * 32)
                        if c == 1 and not first:
                            rows_hi(i - 1)
                    elif last:
                        hi(PLE_N, 2, D)
                    else:
                        hi(DOWN_N, DOWN_ROWS[0][1], CW, (i + 1) * 32)

            down(0, first=True)
            with act.Fori(1, DI - 1) as i:
                down(i)
            down(DI - 1, last=True)

            rows_hi(DI - 1)
            act.wait_ge(sem["proj_done"], PLE_G)
            hi(PLE_N + 1, KD, CW)
            for g in range(8):
                tb, c = g // 2, g % 2
                act.wait_ge(sem["proj_done"], PLE_G + g + 1)
                act.copy(pp[tb][:, S * c:S * c + S], bank[g % 4][:, :]).then_inc(proj_free[g % 4], 1)
            root(2, token_root, bank[MISC][:, 0:NT])
            act.wait_ge(sem["rstd_done"], 2)
            for j in range(4):
                if j < 3:
                    act.wait_ge(sem["proj_done"], PLE_G + 8 + 2 * j)
                    hi(PLE_N + 2 + j, KD, CW)
                for c in range(2):
                    q = 2 * j + c
                    act.wait_ge(sem["proj_done"], PLE_G + 8 + q + 1)
                    if q >= 2:
                        act.wait_ge(sem["out_ready"], q - 1)
                    for i in range(2):
                        ins = act.activation(sig[q % 2][:, i, :], bank[q % 4][:, CW * i:CW * i + CW], ACT.Sigmoid,
                                             scale=token_root[:, 2 * c + i:2 * c + i + 1])
                    ins.then_inc(proj_free[q % 4], 1)

        @block.vector
        def _(dve):
            own = [0]

            def link(ins):
                own[0] += 1
                ins.then_inc(sem["dve_step"], 1)
                dve.wait_ge(sem["dve_step"], own[0])

            dve.memset(st[:, 40:41], EPS)
            dve.memset(st[:, 41:42], 1.0).then_inc(sem["small_done"], 1)

            def norm_sum(d):
                dve.wait_ge(sem["sq_done"], d + 1)
                if d == 0:
                    ins = dve.tensor_copy(sq_sum[:, :], sq[0][:, :])
                else:
                    dve.wait_ge(sem["sum_done"], d)
                    ins = dve.tensor_tensor(sq_sum[:, :], sq_sum[:, :], sq[d % 2][:, :], ALU.add)
                ins.then_inc(sem["sum_done"], 1)

            def scale_tokens(tb):
                dve.wait_ge(sem["token_ss"], tb + 1)
                dve.tensor_scalar(xn[tb][:, :], x_in_sb[tb][:, :], st[:, tb:tb + 1], None, ALU.mult).then_inc(
                    sem["xn_done"], 1)

            def scale_features(q):
                half = q % 2
                dve.wait_ge(sem["xt_done"], q + 1)
                if q >= 4:
                    dve.wait_ge(sem["u_lo_done"], q - 3)
                dve.tensor_tensor(xg[q % 4][:, :, :], bank[QK[q % 2]][:, :].rearrange("p (k c) -> p k c", c=P),
                                  gains[:, 0, 4 * half:4 * half + 4].unsqueeze(2).to_broadcast([P, KD // 2, P]),
                                  ALU.mult).then_inc(sem["normed_done"], 1)

            def u_lo_part(q):
                tb, half = q // 2, q % 2
                r = (slice(None), slice(4 * half, 4 * half + 4), slice(P * tb, P * tb + P))
                dve.wait_ge(sem["u_hi_done"], q + 1)
                dve.tensor_tensor(u_lo[r], xg[q % 4][:, :, :], u_hi[r].bitcast(F32), ALU.subtract).then_inc(
                    sem["u_lo_done"], 1)

            scale_tokens(0)
            dve.wait_ge(sem["vec_turned"], 1)
            link(dve.tensor_copy(vec[:, 0:8], bank[OUT][:, 0:8]))
            scale_tokens(1)
            for q in range(4):
                scale_features(q)
            for q in range(4):
                u_lo_part(q)
            for tb in (2, 3):
                scale_tokens(tb)
                scale_features(2 * tb)
                scale_features(2 * tb + 1)
            for q in range(4, 8):
                u_lo_part(q)
            dve.wait_ge(sem["vec_turned"], 2)
            link(dve.tensor_copy(vec[:, 8:58], bank[MISC][:, 8:58]))
            for i in (54, 56):
                link(dve.tensor_scalar(vec[:, i:i + 1], vec[:, i:i + 1], HD ** -0.5, None, ALU.mult))
            dve.wait_ge(sem["const_in"], 16 * 3)
            dve.wait_ge(sem["rv_mm"], 2)
            dve.tensor_tensor(rv_sb[0:24, 0:S], bank[TR[0]][0:24, :], mask_sb[0:24, 0:S], ALU.add).then_inc(
                sem["rv_done"], 1)
            dve.tensor_tensor(rv_sb[0:24, S:RV], bank[TR[1]][0:24, 0:P], mask_sb[0:24, S:RV], ALU.add).then_inc(
                sem["rv_done"], 1)

            def head_raw(g):
                if g in chain_at:
                    dve.wait_ge(sem["proj_done"], g + 1)
                    dve.tensor_copy(chains[chain_at[g]][1][:, :], bank[bank_of[g]][:, :]).then_inc(
                        proj_free[bank_of[g]], 1)

            def head_scale(g):
                if g - 1 in chain_at:
                    c = chain_at[g - 1]
                    dst = chains[c][1]
                    dve.wait_ge(sem["head_rstd"], c + 1)
                    dve.scalar_tensor_tensor(dst[:, :], dst[:, :], head_gains[:, chains[c][2]:chains[c][2] + 1],
                                             head_tmp[:, :], ALU.mult, ALU.mult).then_inc(sem["head_normed"], 1)

            for g in range(T1_GROUPS):
                head_raw(g)
                head_scale(g)
                if g < KD:
                    dve.wait_ge(sem["xt_done"], KD + g + 1)
                    dve.tensor_copy(hT[:, g, :], bank[QK[g % 2]][:, :]).then_inc(sem["h2_done"], 1)

            def scores(u):
                U = units[u]
                n = len(U["subs"])
                before = u - 2 if u < 16 else u - 4
                if before >= 0 and (u < 16 or before >= 16):
                    V = units[before]
                    dve.wait_ge(sem["t_done"], V["tr0"] + len(V["chunks"]))
                if u < 16:
                    if U["b"] == 0:
                        dve.wait_ge(bias_a_in[u // 4 % 2], 48 * (u // 8 + 1))
                elif U["b"] == 0:
                    h = (u - 16) // 4
                    dve.wait_ge(bias_c_in[h % 4], 16 * (h // 4 + 1))
                for g, sub in enumerate(U["subs"]):
                    k, w = U["qk0"] + g, sub["k1"] - sub["k0"]
                    first = P * (U["b"] + 1) - 1 - sub["k0"]
                    seg, full = U["S"][:, sub["at"]:sub["at"] + w], sub["bias"][:, :]
                    table = bass.AP(tensor=full.tensor, offset=full.offset + first, ap=[[S, P], [-1, w]])
                    dve.wait_ge(sem["qk_done"], k + 1)
                    if u >= 16:
                        ins = dve.tensor_tensor_reduce(seg, bank[QK[k % 2]][:, 0:w], table, -1.0, 3.0e38, ALU.add,
                                                       ALU.min, st_(u, 3))
                        ins.then_inc(qk_free[k % 2], 1)
                    else:
                        ins = dve.tensor_tensor_reduce(seg, bank[QK[k % 2]][:, 0:w], table, -1.0, 3.0e38, ALU.add,
                                                       ALU.min, st_(u, g))
                        ins.then_inc(qk_free[k % 2], 1)
                        if g == n - 1:
                            for q in (k - 1, k):
                                dve.wait_ge(qk_free[q % 2], q // 2 + 1)
                            dve.tensor_reduce(st_(u, 3), st[:, (u % 4) * 8:(u % 4) * 8 + 3],
                                              mybir.AxisListType.X, ALU.min).then_inc(sem["s_ready"], 1)

            def normalise(u):
                U = units[u]
                dve.wait_ge(sem["exp_done"], u + 1)
                link(dve.reciprocal(st_(u, 5), st_(u, 4)))
                dve.tensor_scalar(U["S"][:, 0:U["width"]], U["S"][:, 0:U["width"]], st_(u, 5), None,
                                  ALU.mult).then_inc(sem["p_ready"], 1)

            def out_lo(u):
                if u % 8 == 7:
                    i = pair_tile[u // 8]
                    dve.wait_ge(sem["o_hi_done"], u // 8 + 1)
                    dve.tensor_tensor(s_lo[:, i, :], out_bank(u)[:, :], s_hi[:, i, :].bitcast(F32),
                                      ALU.subtract).then_inc(sem["o_lo_done"], 1)

            for i in range(18):
                if i < 16:
                    scores(i)
                if 1 <= i <= 16:
                    normalise(i - 1)
                if i >= 3:
                    out_lo(i - 3)
                g = T1_GROUPS + i
                if g <= T2_GROUPS:
                    head_scale(g)
                if g < T2_GROUPS:
                    key, j = kind_of[g]
                    b_ = bank_of[g]
                    if key in ("iq", "ik", "al"):
                        dst = iq[j] if key == "iq" else ik if key == "ik" else al
                        r = slice(0, AVI if key == "al" else P)
                        dve.wait_ge(sem["proj_done"], g + 1)
                        dve.tensor_copy(dst[r, :], bank[b_][r, :]).then_inc(proj_free[b_], 1)
                    if key == "cviw":
                        v = bank[b_][:, 0:NT * AVI].rearrange("p (t c) -> p t c", t=NT)
                        dve.wait_ge(sem["proj_done"], g + 1)
                        dve.tensor_copy(cv[:, :, :], v[:, :, 16:16 + HD])
                        dve.tensor_scalar(iw[:, :, :], v[:, :, 16 + HD:AVI], IDX_HEADS ** -0.5 * HD ** -0.5, None,
                                          ALU.mult).then_inc(proj_free[b_], 1)
                if g < T2_GROUPS:
                    head_raw(g)
            out_lo(15)

            for e, (b, h) in enumerate(idx):
                w = P * (b + 1)
                dve.wait_ge(sem["qk_done"], IDX_QK0 + e + 1)
                dve.wait_ge(qk_free[(IDX_QK0 + e) % 2], (IDX_QK0 + e) // 2 + 1)
                if e:
                    dve.wait_ge(sem["relu_used"], e)
                if h == 0:
                    ins = dve.tensor_scalar(score[b][:, 0:w], relu[e % 2][:, 0:w], iw[:, b, h:h + 1], None, ALU.mult)
                else:
                    ins = dve.scalar_tensor_tensor(score[b][:, 0:w], relu[e % 2][:, 0:w], iw[:, b, h:h + 1],
                                                   score[b][:, 0:w], ALU.mult, ALU.add)
                ins.then_inc(sem["relu_used"], 1)
            dve.wait_ge(sem["relu_used"], 24)
            steps = [0]

            def topk_step(ins, b):
                ins.then_inc(sem["topk_done"], 1)
                steps[0] += 1
                done[b] = steps[0]

            done = {}
            for b in (1, 2, 3):
                topk_step(dve.tensor_tensor(score[b][:, P * b:P * b + P], score[b][:, P * b:P * b + P], hidden,
                                            ALU.add), b)
            for r in range(TOPK // 8):
                for b in (1, 2, 3):
                    dve.wait_ge(sem["topk_done"], done[b])
                    topk_step(dve.max(top8[:, b - 1, :], score[b][:, 0:P * (b + 1)]), b)
                for b in (1, 2, 3):
                    dve.wait_ge(sem["topk_done"], done[b])
                    topk_step(dve.match_replace(score[b][:, 0:P * (b + 1)], top8[:, b - 1, :],
                                                score[b][:, 0:P * (b + 1)], TAKEN), b)
            for b in (1, 2, 3):
                dve.wait_ge(sem["topk_done"], done[b])
                dve.tensor_scalar(chosen[b][:, 0:P * (b + 1)], score[b][:, 0:P * (b + 1)],
                                  (HIDDEN + TAKEN) / 2, NEG, ALU.is_gt, ALU.mult).then_inc(sem["sel_done"], 1)
            dve.tensor_copy(ident_r[:, :], ident).then_inc(sem["sel_done"], 1)

            for j in range(53):
                if j < 48:
                    scores(16 + j)
                if 2 <= j <= 49:
                    normalise(16 + j - 2)
                if j >= 5:
                    out_lo(16 + j - 5)

            link(dve.memset(g_reset[:, :], 1.0))
            dve.memset(g_reset[:, 0:S:CH], 0.0).then_inc(sem["reset_done"], 1)
            dve.wait_ge(sem["reset_done"], 1)

            def gla(h, stage):
                if stage == 0:
                    lf, cum = g_t[1], g_t[2]
                    dve.wait_ge(sem["gl_abs"], h + 1)
                    link(dve.tensor_scalar(lf[:, :], bank[2][:, :], ba[:, h:h + 1], 0.0, ALU.add, ALU.min))
                    dve.wait_ge(sem["gl_ln"], h + 1)
                    link(dve.tensor_tensor(lf[:, :], lf[:, :], g_t[0][:, :], ALU.subtract))
                    dve.tensor_tensor_scan(cum[:, :], g_reset[:, :], lf[:, :], 0.0, ALU.mult, ALU.add).then_inc(
                        sem["gl_min"], 1)
                    dve.wait_ge(sem["gl_min"], h + 1)
                    last = cum[:, CH - 1:S:CH]
                    dve.tensor_tensor(g_t[0][:, :].rearrange("p (n c) -> p n c", c=CH),
                                      last.unsqueeze(2).to_broadcast([P, NCH, CH]),
                                      cum[:, :].rearrange("p (n c) -> p n c", c=CH), ALU.subtract).then_inc(
                        sem["gl_scan"], 1)
                    dve.wait_ge(sem["gl_e"], 4 * h + 1)
                    dve.scalar_tensor_tensor(bqk[2 * h][:, :], bqk[2 * h][:, :], float(P) ** -0.5, g_t[3][:, :],
                                             ALU.mult, ALU.mult).then_inc(sem["gl_qk"], 1)
                    dve.wait_ge(sem["gl_e"], 4 * h + 2)
                    dve.tensor_tensor(g_t[5][:, :], bqk[2 * h + 1][:, :], g_t[4][:, :], ALU.mult).then_inc(
                        sem["gl_qk"], 1)
                    dve.wait_ge(sem["gl_e"], 4 * h + 3)
                    dve.tensor_tensor(bqk[2 * h + 1][:, :], bqk[2 * h + 1][:, :], g_t[1][:, :], ALU.mult).then_inc(
                        sem["gl_qk"], 1)
                elif stage == 1:
                    dve.wait_ge(sem["gl_att"], h + 1)
                    dve.tensor_tensor(g_t[3][:, :].rearrange("p (n c) -> p n c", c=P),
                                      bank[3][:, :].rearrange("p (n c) -> p n c", c=P),
                                      chunk_causal.unsqueeze(1).to_broadcast([P, NT, P]), ALU.mult).then_inc(
                        sem["gl_attT"], 1)
                elif stage == 2:
                    dve.wait_ge(sem["gl_e"], 4 * h + 4)
                    for c in range(NCH - 1):
                        dst = g_state[c // 2][:, c % 2, :]
                        src = bank[TR[c % 2]][:, 0:GV]
                        dve.wait_ge(sem["gl_u"], (NCH - 1) * h + c + 1)
                        if c == 0:
                            ins = dve.tensor_copy(dst, src)
                        else:
                            ins = dve.scalar_tensor_tensor(dst, g_state[(c - 1) // 2][:, (c - 1) % 2, :],
                                                           decay[:, c:c + 1], src, ALU.mult, ALU.add)
                        ins.then_inc(sem["gl_state"], 1)
                        dve.wait_ge(sem["gl_state"], (NCH - 1) * h + c + 1)
                elif stage == 4:
                    dve.wait_ge(sem["gl_r"], h + 1)
                    for e in range(2):
                        dve.scalar_tensor_tensor(bqk[2 * h + e][:, :], g_t[4 + e][:, :], gg[:, e:e + 1],
                                                 g_t[2][:, :], ALU.mult, ALU.mult).then_inc(sem["gl_out"], 1)

            def gate(g):
                key, d = kind_of[g]
                b_ = bank_of[g]
                if key == "ya":
                    dve.wait_ge(proj_free[bank_of[g_of["ga", d]]], use_of[g_of["ga", d]] + 1)
                    dve.wait_ge(sem["proj_done"], g + 1)
                    dve.tensor_tensor(part[d][:, :], part[d][:, :], bank[b_][:, :], ALU.mult).then_inc(
                        proj_free[b_], 1)
                    dve.wait_ge(proj_free[b_], use_of[g] + 1)
                elif key == "yc":
                    dve.wait_ge(proj_free[bank_of[g_of["gc", d]]], use_of[g_of["gc", d]] + 1)
                    dve.wait_ge(sem["proj_done"], g + 1)
                    dve.tensor_tensor(gate_t[d % 2][:, :], gate_t[d % 2][:, :], bank[b_][:, :], ALU.mult).then_inc(
                        proj_free[b_], 1)
                    dve.wait_ge(proj_free[b_], use_of[g] + 1)
                    dve.tensor_tensor(part[d][:, :], part[d][:, :], gate_t[d % 2][:, :], ALU.add).then_inc(
                        sem["part_done"], 1)
                elif key == "br":
                    tmp = silu_r[d % 4]
                    dve.wait_ge(proj_free[b_], use_of[g] + 1)
                    dve.wait_ge(sem["gl_out"], d + 1)
                    dve.tensor_tensor(tmp[:, :], tmp[:, :], bqk[d][:, :], ALU.mult).then_inc(sem["r_prod"], 1)
                elif key == "yb":
                    tmp = gate_b_t[d % 4]
                    dve.wait_ge(proj_free[bank_of[g_of["gb", d]]], use_of[g_of["gb", d]] + 1)
                    dve.wait_ge(sem["proj_done"], g + 1)
                    dve.tensor_tensor(tmp[:, :], tmp[:, :], bank[b_][:, :], ALU.mult).then_inc(proj_free[b_], 1)
                    dve.wait_ge(proj_free[b_], use_of[g] + 1)
                    dve.tensor_tensor(tmp[:, :], tmp[:, :], part[d][:, :], ALU.add).then_inc(sem["m_sum"], 1)

            for j in range(STEPS):
                gla(j // 5, j % 5)
                for g in t4_step[j]:
                    gate(g)

            def r_lo(d):
                dve.wait_ge(sem["r_hi"], d + 1)
                dve.tensor_tensor(s_lo[:, 2 + d, :], silu_r[d % 4][:, :], s_hi[:, 2 + d, :].bitcast(F32),
                                  ALU.subtract).then_inc(sem["r_lo"], 1)

            def m_lo(d):
                dve.wait_ge(sem["m_hi"], d + 1)
                dve.tensor_tensor(merged[d][1], gate_b_t[d % 4][:, :], merged[d][0].bitcast(F32),
                                  ALU.subtract).then_inc(sem["m_lo"], 1)

            for g in range(T4_GROUPS, g_of["wo", 0]):
                key, d = kind_of[g]
                if key == "gb" and d == 0:
                    r_lo(KD - 1)
                gate(g)
                if key == "br" and d >= 1:
                    r_lo(d - 1)
                if key == "yb":
                    m_lo(d)
            for d in range(KD):
                g = g_of["wo", d]
                dve.wait_ge(sem["proj_done"], g + 1)
                dve.tensor_tensor(hT[:, d, :], hT[:, d, :], bank[bank_of[g]][:, :], ALU.add).then_inc(
                    sem["h2_done"], 1)
                dve.wait_ge(sem["h2_done"], KD + d + 1)
                if d >= 2:
                    dve.wait_ge(sem["u_lo_done"], KD + d - 1)
                dve.tensor_scalar(normed[d % 2][:, :], hT[:, d, :], gains[:, 1, d:d + 1], None,
                                  ALU.mult).then_inc(sem["normed_done"], 1)
                if d:
                    norm_sum(d - 1)
                dve.wait_ge(sem["u_hi_done"], KD + d + 1)
                dve.tensor_tensor(u_lo[:, d, :], normed[d % 2][:, :], u_hi[:, d, :].bitcast(F32),
                                  ALU.subtract).then_inc(sem["u_lo_done"], 1)
            norm_sum(KD - 1)
            dve.wait_ge(sem["rstd_done"], 1)

            def ffn(i, first=False):
                for c in range(2):
                    dve.wait_ge(sem["proj_done"], i * 4 + (FFN_G + 1 + c))
                    if not first:
                        dve.wait_ge(proj_free[2 + c], i + uses[2 + c])
                    dve.tensor_tensor(silu_g[c][:, :], bank[c][:, :], rstd[:, :], ALU.mult).then_inc(proj_free[c], 1)
                for c in range(2):
                    dve.wait_ge(sem["ff_silu"], i * 2 + (c + 1))
                    dve.tensor_tensor(silu_g[c][:, :], silu_g[c][:, :], rstd[:, :], ALU.mult).then_inc(
                        sem["ff_scaled"], 1)
                if not first:
                    dve.wait_ge(sem["ff_lo"], i * 2)
                def lo(c):
                    dve.wait_ge(sem["ff_hi"], i * 2 + (c + 1))
                    dve.tensor_tensor(s_lo[:, bass.ds(i * 2 + c, 1), :], prod[c][:, :, :],
                                      s_hi[:, bass.ds(i * 2 + c, 1), :].bitcast(F32),
                                      ALU.subtract).then_inc(sem["ff_lo"], 1)

                for c in range(2):
                    dve.wait_ge(sem["proj_done"], i * 4 + (FFN_G + 3 + c))
                    dve.wait_ge(sem["ff_scaled"], i * 2 + (c + 1))
                    dve.tensor_tensor(prod[c][:, 0, :], silu_g[c][:, :], bank[2 + c][:, :], ALU.mult).then_inc(
                        proj_free[2 + c], 1)
                for c in range(2):
                    lo(c)

            ffn(0, first=True)
            with dve.Fori(1, FI) as i:
                ffn(i)

            for k in range(2):
                dve.wait_ge(sem["p_hi"], k + 1)
                dve.tensor_tensor(p_lo[:, k, :], bank[TR[k]][:, :], p_hi[:, k, :].bitcast(F32),
                                  ALU.subtract).then_inc(sem["p_lo"], 1)

            dve.wait_ge(sem["ff_lo"], KF)
            link(dve.memset(sq_sum[:, :], 0.0))
            with dve.Fori(0, DI) as i:
                for c in range(2):
                    dve.wait_ge(sem["proj_done"], i * 2 + (DOWN_G + c + 1))
                    row = hT[:, bass.ds(i * 2 + c, 1), :]
                    dve.tensor_tensor(row, row, bank[c][:, :].unsqueeze(1), ALU.add).then_inc(sem["h2_done"], 1)
                    dve.wait_ge(sem["h2_done"], i * 2 + (2 * KD + c + 1))
                    dve.wait_ge(sem["u_lo_done"], i * 2 + (2 * KD + c - 1))
                    dve.tensor_tensor(normed_row[c][:, :, :], row,
                                      gains[:, 2, bass.ds(i * 2 + c, 1)].unsqueeze(2).to_broadcast([P, 1, S]),
                                      ALU.mult).then_inc(sem["normed_done"], 1)
                for c in range(2):
                    dve.wait_ge(sem["u_hi_done"], i * 2 + (2 * KD + c + 1))
                    dve.tensor_tensor(u_lo[:, bass.ds(i * 2 + c, 1), :], normed_row[c][:, :, :],
                                      u_hi[:, bass.ds(i * 2 + c, 1), :].bitcast(F32),
                                      ALU.subtract).then_inc(sem["u_lo_done"], 1)
                    dve.wait_ge(sem["sq_done"], i * 2 + (KD + c + 1))
                    dve.wait_ge(sem["sum_done"], i * 2 + (KD + c))
                    dve.tensor_tensor(sq_sum[:, :], sq_sum[:, :], sq_row[c][:, 0, :], ALU.add).then_inc(
                        sem["sum_done"], 1)

            for j in range(4):
                for c in range(2):
                    q = 2 * j + c
                    dve.wait_ge(proj_free[q % 4], ple_free(8 + q) + 1)
                    sg = sig[q % 2]
                    for i in range(2):
                        ins = dve.tensor_tensor(sg[:, i, :], sg[:, i, :], pp[2 * c + i][:, CW * j:CW * j + CW],
                                                ALU.mult)
                    link(ins)
                    dve.wait_ge(sem["ht_done"], q + 1)
                    dve.tensor_tensor(out_sb[q][:, :, :], sg[:, :, :],
                                      bank[TR[q % 2]][:, :].rearrange("p (t c) -> p t c", t=2),
                                      ALU.add).then_inc(sem["out_ready"], 1)

        @block.tensor
        def _(pe):
            def mm3(dst, w, x, start, stop):
                (wh, wl), (xh, xl) = w, x
                pe.matmul(dst, wh, xh, start=start, stop=False)
                pe.matmul(dst, wh, xl, start=False, stop=False)
                return pe.matmul(dst, wl, xh, start=False, stop=stop)

            def project(g):
                G = groups[g]
                n, b_ = G["slot"], bank_of[g]
                kc, width, _ = slots[n]
                wh, wl = part_views(n, kc, width)
                if first_group[n] == g:
                    pe.wait_ge(sem["lo_ready"], n + 1)
                if use_of[g]:
                    pe.wait_ge(proj_free[b_], use_of[g])
                if kind_of[g][0] == "wo" and kind_of[g][1] >= 4:
                    pe.wait_ge(sem["h2_done"], KD + kind_of[g][1] - 3)
                if G["kind"] == "turn":
                    a = g_of["al", 0]
                    pe.wait_ge(proj_free[bank_of[a]], use_of[a] + 1)
                    for tb in range(NT):
                        last = pe.transpose(bank[b_][:, AVI * tb:AVI * tb + AVI], al[0:AVI, P * tb:P * tb + P],
                                            ident[0:AVI, 0:AVI])
                elif G["kind"] == "feat":
                    c = slice(G["c0"], G["c0"] + G["m"])
                    for k in range(kc):
                        if kind_of[g] == ("wo", 0):
                            pe.wait_ge(sem["m_lo"], k + 1)
                        last = mm3(bank[b_][0:G["m"], :], (wh[:, k, c], wl[:, k, c]), G["x"](k), k == 0, k == kc - 1)
                else:
                    w = G["n"]
                    c = slice(G["c0"], G["c0"] + w)
                    for i, tb in enumerate(G["toks"]):
                        r = slice(P * tb, P * tb + P)
                        for k in range(kc):
                            last = mm3(bank[b_][:, w * i:w * i + w], (u_hi[:, k, r], u_lo[:, k, r]),
                                       (wh[:, k, c], wl[:, k, c]), k == 0, k == kc - 1)
                last.then_inc(sem["proj_done"], 1)

            pe.wait_ge(sem["mix_in"], MIX)
            pe.transpose(bank[OUT][:, 0:8], vec_rows[0:8, 0:P], ident[0:8, 0:8]).then_inc(sem["vec_turned"], 1)
            for q in range(8):
                tb, half = q // 2, q % 2
                if q >= 2:
                    pe.wait_ge(sem["normed_done"], q - 1)
                pe.wait_ge(sem["xn_done"], tb + 1)
                for k in range(4):
                    d = 4 * half + k
                    last = pe.transpose(bank[QK[q % 2]][:, P * k:P * k + P], xn[tb][:, P * d:P * d + P], ident)
                last.then_inc(sem["xt_done"], 1)
            pe.wait_ge(sem["vec_in"], VECS)
            pe.transpose(bank[MISC][:, 0:58], vec_rows[0:58, 0:P], ident[0:58, 0:58]).then_inc(sem["vec_turned"], 1)
            pe.wait_ge(sem["const_in"], 16 * 3)
            for h_, (a, b) in enumerate(((0, S), (S, RV))):
                pe.matmul(bank[TR[h_]][0:24, 0:b - a], relb_sb[0:BUCKETS, 0:24], onehot_sb[0:BUCKETS, a:b],
                          start=True, stop=True).then_inc(sem["rv_mm"], 1)

            def turn_x(d):
                pe.wait_ge(sem["normed_done"] if d < 2 else sem["h2_done"], 7 + d if d < 2 else d - 1)
                for tb in range(NT):
                    last = pe.transpose(bank[QK[d % 2]][:, P * tb:P * tb + P], x_in_sb[tb][:, P * d:P * d + P], ident)
                last.then_inc(sem["xt_done"], 1)

            def head_sum(g):
                if g in chain_at:
                    c = chain_at[g]
                    pe.wait_ge(sem["head_sq"], c + 1)
                    pe.matmul(bank[MISC][:, :], head_ones, head_tmp[:, :], start=True, stop=True).then_inc(
                        sem["head_ss"], 1)

            for g in range(T1_GROUPS):
                if g < 2:
                    pe.wait_ge(sem["u_lo_done"], 4 * g + 4)
                project(g)
                head_sum(g - 1)
                if g < KD:
                    turn_x(g)

            def qk(u):
                U = units[u]
                r = slice(HD * U["half"], HD * U["half"] + HD)
                for g, sub in enumerate(U["subs"]):
                    k = U["qk0"] + g
                    if k >= 2:
                        pe.wait_ge(qk_free[k % 2], k // 2)
                    dst, masked = bank[QK[k % 2]][:, 0:sub["k1"] - sub["k0"]], u >= 16 and U["b"] > 0
                    last = pe.matmul(dst, sub["q"][r, P * U["b"]:P * U["b"] + P], sub["k"][r, sub["k0"]:sub["k1"]],
                                     start=True, stop=not masked)
                    if masked:
                        last = pe.matmul(dst, ident_r[:, :], chosen[U["b"]][:, 0:sub["k1"]], start=False, stop=True)
                    last.then_inc(sem["qk_done"], 1)

            def turn(u):
                U = units[u]
                pe.wait_ge(sem["p_ready"], u + 1)
                for c, ch in enumerate(U["chunks"]):
                    k = U["tr0"] + c
                    if k >= 2:
                        pe.wait_ge(sem["t_free"], k - 1)
                    for i, (at, _) in enumerate(ch):
                        last = pe.transpose(bank[TR[k % 2]][:, P * i:P * i + P], U["S"][:, at:at + P], ident)
                    last.then_inc(sem["t_done"], 1)

            def values(u):
                U = units[u]
                pe.wait_ge(sem["t_free"], U["tr0"] + len(U["chunks"]))
                if u % 8 == 0 and u:
                    pe.wait_ge(sem["o_lo_done"], u // 8 - (u >= 24))
                flat = [v for ch in U["chunks"] for _, v in ch]
                r = slice(HD * U["half"], HD * U["half"] + HD)
                for i, v in enumerate(flat):
                    last = pe.matmul(out_bank(u)[r, P * U["b"]:P * U["b"] + P], v, U["PT"][:, P * i:P * i + P],
                                     start=(i == 0), stop=(i == len(flat) - 1))
                last.then_inc(sem["pv_done"], 1)

            pe.wait_ge(sem["head_normed"], 12)
            for i in range(18):
                if i < 16:
                    qk(i)
                if i < 16:
                    if T1_GROUPS + i <= T2_GROUPS:
                        head_sum(T1_GROUPS + i - 1)
                    project(T1_GROUPS + i)
                if 1 <= i <= 16:
                    turn(i - 1)
                if i >= 2:
                    values(i - 2)

            for e, (b, h) in enumerate(idx):
                k = IDX_QK0 + e
                r = slice(HD * (h % 2), HD * (h % 2) + HD)
                pe.wait_ge(qk_free[k % 2], k // 2)
                pe.matmul(bank[QK[k % 2]][:, 0:P * (b + 1)], iq[h // 2][r, P * b:P * b + P], ik[r, 0:P * (b + 1)],
                          start=True, stop=True).then_inc(sem["qk_done"], 1)
                if e % 6 == 5:
                    project(T2_GROUPS + 2 + e // 6)
            for g in range(T2_GROUPS + 6, B_IN_C):
                project(g)
            pe.wait_ge(sem["head_normed"], len(chains))
            pe.wait_ge(sem["sel_done"], 4)
            qk(16)
            for j in range(53):
                if j + 1 < 48:
                    qk(16 + j + 1)
                if j % 2 == 0 and B_IN_C + j // 2 < T3_GROUPS:
                    project(B_IN_C + j // 2)
                if 3 <= j <= 50:
                    turn(16 + j - 3)
                if j in EARLY:
                    project(T3_GROUPS + EARLY.index(j))
                if 4 <= j <= 51:
                    values(16 + j - 4)

            pe.wait_ge(qk_free[0], (n_qk + 1) // 2)
            for b_ in range(2):
                pe.wait_ge(proj_free[b_], use_of[T3_GROUPS - 2 + b_] + 1)

            def gla(h, stage):
                if stage == 0:
                    if h:
                        pe.wait_ge(sem["gl_r"], h)
                    pe.wait_ge(sem["wa2_in"], 16 * (h + 1))
                    pe.matmul(bank[2][:, :], wa2_sb[0:16, :], al[0:16, :], start=True,
                              stop=True).then_inc(sem["gl_L"], 1)
                elif stage == 1:
                    pe.wait_ge(sem["gl_qk"], 3 * h + 2)
                    for tb in range(NT):
                        r = slice(P * tb, P * tb + P)
                        last = pe.matmul(bank[3][:, r], g_t[5][:, r], bqk[2 * h][:, r], start=True, stop=True)
                    last.then_inc(sem["gl_att"], 1)
                    pe.wait_ge(sem["gl_qk"], 3 * h + 3)
                    for tb in range(NT):
                        last = pe.transpose(bank[2][:, P * tb:P * tb + P], bqk[2 * h + 1][:, P * tb:P * tb + P], ident)
                    last.then_inc(sem["gl_tk"], 1)
                elif stage == 2:
                    pe.wait_ge(sem["gl_kend"], h + 1)
                    for c in range(NCH - 1):
                        q = (NCH - 1) * h + c
                        if q >= 2:
                            pe.wait_ge(sem["gl_state"], q - 1)
                        r = slice(CH * (c % 2), CH * (c % 2) + CH)
                        pe.matmul(bank[TR[c % 2]][:, 0:GV], g_t[1][r, P * (c // 2):P * (c // 2) + P],
                                  bv[c // 2][r, GV * h:GV * h + GV], start=True, stop=True).then_inc(sem["gl_u"], 1)
                elif stage == 3:
                    pe.wait_ge(sem["o_lo_done"], 8)
                    pe.wait_ge(sem["gl_attT"], h + 1)
                    pe.wait_ge(sem["gl_state"], (NCH - 1) * (h + 1))
                    for e in range(2):
                        b_ = bank[(OUT, MISC)[e]]
                        if h:
                            pe.wait_ge(sem["gl_osq"], 4 * (h - 1) + 2 * e + 1)
                        for tb in range(NT):
                            r = slice(P * tb, P * tb + P)
                            last = pe.matmul(b_[:, r], bv[tb][:, GV * h + P * e:GV * h + P * e + P], g_t[3][:, r],
                                             start=True, stop=False)
                            for c in (2 * tb, 2 * tb + 1):
                                if c:
                                    q = slice(CH * c, CH * c + CH)
                                    last = pe.matmul(b_[:, q], g_state[(c - 1) // 2][:, (c - 1) % 2, P * e:P * e + P],
                                                     bqk[2 * h][:, q], start=False, stop=(c % 2 == 1))
                        last.then_inc(sem["gl_o"], 1)
                else:
                    for e in range(2):
                        pe.wait_ge(sem["gl_osq"], 4 * h + 2 * e + 2)
                        last = pe.matmul(bank[2][:, :], ones, g_t[e][:, :], start=(e == 0), stop=(e == 1))
                    last.then_inc(sem["gl_ss"], 1)

            for j in range(STEPS):
                gla(j // 5, j % 5)
                for g in t4_step[j]:
                    if kind_of[g] == ("yc", 0):
                        pe.wait_ge(sem["o_lo_done"], 8)
                    project(g)

            for g in range(T4_GROUPS, PRE_GROUPS):
                key, d = kind_of[g]
                if key == "yb" and d == 0:
                    pe.wait_ge(sem["r_lo"], KD)
                project(g)

            def ffn(i, first=False):
                for half in range(2):
                    n = FFN_N + half
                    wh, wl = part_views(n, KD, CW)
                    pe.wait_ge(sem["lo_ready"], i * 2 + (n + 1))
                    for c in range(2):
                        b_ = 2 * half + c
                        pe.wait_ge(proj_free[b_], i + uses[b_])
                        for k in range(KD):
                            if first and half == 0 and c == 0:
                                pe.wait_ge(sem["u_lo_done"], KD + k + 1)
                            last = mm3(bank[b_][:, :], (wh[:, k, P * c:P * c + P], wl[:, k, P * c:P * c + P]),
                                       u_tile(k), k == 0, k == KD - 1)
                        last.then_inc(sem["proj_done"], 1)
                        if first and half == 0 and c == 0:
                            pe.wait_ge(sem["sum_done"], KD)
                            pe.matmul(bank[MISC][:, :], ones, sq_sum[:, :], start=True, stop=True).then_inc(
                                sem["ss_done"], 1)

            ffn(0, first=True)
            with pe.Fori(1, FI) as i:
                ffn(i)

            pe.wait_ge(sem["p_in"], 16)
            for k in range(2):
                for tb in range(NT):
                    last = pe.transpose(bank[TR[k]][:, P * tb:P * tb + P], p_sb[:, tb, P * k:P * k + P], ident)
                last.then_inc(sem["pt_done"], 1)

            for b_ in range(4):
                pe.wait_ge(proj_free[b_], uses[b_] + FI)

            def down(i, first=False):
                for j, (k0, kc) in enumerate(DOWN_ROWS):
                    n = DOWN_N + j
                    wh, wl = part_views(n, kc, CW)
                    pe.wait_ge(sem["lo_ready"], i * 4 + (n + 1))
                    for c in range(2):
                        if j == 0:
                            pe.wait_ge(sem["h2_done"], i * 2 + (2 * KD - 1 + c))
                        for k in range(kc):
                            if first and c == 0:
                                pe.wait_ge(sem["ff_lo"], k0 + k + 1)
                            last = mm3(bank[c][:, :], (wh[:, k, P * c:P * c + P], wl[:, k, P * c:P * c + P]),
                                       o_tile(k0 + k), j == 0 and k == 0, j == 3 and k == kc - 1)
                        if j == 3:
                            last.then_inc(sem["proj_done"], 1)
                    if j < 3:
                        last.then_inc(sem["w_used"], 1)

            down(0, first=True)
            with pe.Fori(1, DI) as i:
                down(i)

            pe.wait_ge(sem["p_lo"], 2)
            wh, wl = part_views(PLE_N, 2, D)
            pe.wait_ge(sem["lo_ready"], PLE_N + 1)
            for g in range(8):
                tb, c = g // 2, g % 2
                r, q = slice(P * tb, P * tb + P), slice(S * c, S * c + S)
                if g < 2:
                    pe.wait_ge(sem["h2_done"], 3 * KD - 1 + g)
                pe.wait_ge(proj_free[g % 4], ple_free(g))
                for k in range(2):
                    last = mm3(bank[g % 4][:, :], (p_hi[:, k, r], p_lo[:, k, r]), (wh[:, k, q], wl[:, k, q]),
                               k == 0, k == 1)
                last.then_inc(sem["proj_done"], 1)
            pe.wait_ge(sem["sum_done"], 2 * KD)
            for tb in range(NT):
                last = pe.matmul(bank[MISC][:, tb:tb + 1], sq_sum[:, P * tb:P * tb + P], ones[:, 0:1], start=True,
                                 stop=True)
            last.then_inc(sem["ss_done"], 1)
            pe.wait_ge(sem["u_lo_done"], 3 * KD)
            for j in range(4):
                wh, wl = part_views(PLE_N + 1 + j, KD, CW)
                pe.wait_ge(sem["lo_ready"], PLE_N + 2 + j)
                for c in range(2):
                    q = 2 * j + c
                    pe.wait_ge(proj_free[q % 4], ple_free(8 + q))
                    for i in range(2):
                        r = slice(P * (2 * c + i), P * (2 * c + i) + P)
                        for k in range(KD):
                            last = mm3(bank[q % 4][:, CW * i:CW * i + CW], (u_hi[:, k, r], u_lo[:, k, r]),
                                       (wh[:, k, :], wl[:, k, :]), k == 0, k == KD - 1)
                    last.then_inc(sem["proj_done"], 1)
                    if q >= 2:
                        pe.wait_ge(sem["out_ready"], q - 1)
                    for i in range(2):
                        r = slice(P * (2 * c + i), P * (2 * c + i) + P)
                        for dd in range(2):
                            last = pe.transpose(bank[TR[q % 2]][:, CW * i + P * dd:CW * i + P * dd + P],
                                                hT[:, 2 * j + dd, r], ident)
                    last.then_inc(sem["ht_done"], 1)


_INS = ["x", "p", "rel_bias", "norm_mix", "w_in", "qn_a", "kn_a", "qn_c", "kn_c", "w_alpha2", "b_alpha", "gla_norm",
        "w_out_a", "w_out_b", "w_out_c", "w_gate", "b_gate", "w_o", "norm_ffn", "w_ffn_gate", "w_ffn_up",
        "w_ffn_down", "norm_ple", "w_ple_gate", "w_ple_proj"]


def kernel(**inputs):
    import concourse.bacc as bacc
    from concourse.bass_utils import run_bass_kernel_spmd

    nc = bacc.Bacc("TRN2", target_bir_lowering=False, num_devices=1)
    arrays = {name: np.ascontiguousarray(inputs[name]) for name in _INS}
    arrays["c_onehot"], arrays["c_mask"], arrays["c_tables"] = shape_tables()
    aps = {name: nc.dram_tensor(name, a.shape, mybir.dt.from_np(a.dtype), kind="ExternalInput").ap()
           for name, a in arrays.items()}
    aps["c_scratch"] = nc.dram_tensor("c_scratch", (24, RV), F32, kind="Internal").ap()
    out = nc.dram_tensor("out", (1, S, D), F32, kind="ExternalOutput").ap()
    build(nc, aps, out)
    r = run_bass_kernel_spmd(nc, [arrays], core_ids=[0])
    return r.results[0]["out"]
```
